# Optimizing a Trainium2 kernel written in Bass

```python
import jax, jax.numpy as jnp
from jax import lax
import numpy as np

D_MODEL = 1024
BATCH = 1
SEQ = 128
DEPTH = 2
DEC_BATCH = 1
DEC_SEQ = 128
PAST_LEN = 128

GRID_W = 64
ROPE_THETA = 10000.0
BLOCK_Q = 128
WINDOW = 128
HD = 64
H_A = 8
NOPE_A = 64
ROPE_A = 32
V_A = 64
Q_LORA = 256
KV_LORA = 128
H_B = 8
KVH_B = 2
H_C = 16
KVH_C = 4
AB_IN = Q_LORA + KV_LORA + ROPE_A + H_B * HD + 2 * KVH_B * HD
AB_OUT = H_A * V_A + H_B * HD
C_IN = H_C * HD + 2 * KVH_C * HD
C_OUT = H_C * HD
N_EXPERTS = 16
N_GROUPS = 4
EXPERTS_PER_GROUP = N_EXPERTS // N_GROUPS
TOP_K = 2
D_EXPERT = 512
ALPHA = (2 * DEPTH) ** 0.25
BETA = (8 * DEPTH) ** -0.25
N_EVEN = (DEPTH + 1) // 2
N_ODD = DEPTH // 2
NEG_INF = -1e30
EPS = 1e-6

kernel_name = "hybrid_mla_swa_gqa_moe_diffusion_step"

def rms_norm(x, g):
    xf = x.astype(jnp.float32)
    y = xf * lax.rsqrt(jnp.mean(xf * xf, axis=-1, keepdims=True) + EPS)
    return (y * g.astype(jnp.float32)).astype(x.dtype)

def layer_norm(x, g, b):
    xf = x.astype(jnp.float32)
    mu = jnp.mean(xf, axis=-1, keepdims=True)
    xc = xf - mu
    var = jnp.mean(xc * xc, axis=-1, keepdims=True)
    y = xc * lax.rsqrt(var + EPS) * g.astype(jnp.float32) + b.astype(jnp.float32)
    return y.astype(x.dtype)

def grid_angles(n_tok, rot_dim):
    rows = n_tok // GRID_W
    row = jnp.repeat(jnp.arange(rows, dtype=jnp.float32), GRID_W)
    col = jnp.tile(jnp.arange(GRID_W, dtype=jnp.float32), rows)
    n_freq = rot_dim // 4
    inv = 1.0 / (ROPE_THETA ** (jnp.arange(n_freq, dtype=jnp.float32) / n_freq))
    ang = jnp.concatenate([row[:, None] * inv, col[:, None] * inv], axis=-1)
    return jnp.cos(ang), jnp.sin(ang)

def apply_rope(x, cos, sin):
    half = x.shape[-1] // 2
    shp = (1, x.shape[1]) + (1,) * (x.ndim - 3) + (half,)
    cos = cos.reshape(shp)
    sin = sin.reshape(shp)
    x1 = x[..., :half].astype(jnp.float32)
    x2 = x[..., half:].astype(jnp.float32)
    return jnp.concatenate([x1 * cos - x2 * sin, x2 * cos + x1 * sin], axis=-1).astype(x.dtype)

def softmax_attend(q, k, v, sink=None):
    scale = q.shape[-1] ** -0.5
    s = jnp.einsum("bqhgd,bkhd->bhgqk", q, k).astype(jnp.float32) * scale
    if sink is not None:
        hk, g = q.shape[2], q.shape[3]
        s_sink = jnp.broadcast_to(sink.reshape(1, hk, g, 1, 1).astype(jnp.float32), s.shape[:-1] + (1,))
        s = jnp.concatenate([s, s_sink], axis=-1)
    p = jax.nn.softmax(s, axis=-1)[..., :k.shape[1]].astype(v.dtype)
    return jnp.einsum("bhgqk,bkhd->bqhgd", p, v)

def block_sweep(q, k, v, sink=None):
    b, t = q.shape[:2]
    nb = t // BLOCK_Q
    qb = jnp.swapaxes(q.reshape((b, nb, BLOCK_Q) + q.shape[2:]), 0, 1)
    ob = lax.map(lambda qi: softmax_attend(qi, k, v, sink), qb)
    return jnp.swapaxes(ob, 0, 1).reshape((b, t) + ob.shape[3:])

def band_attend(q, k, v, k_ctx, v_ctx, sink):
    b, t, hk, g, d = q.shape
    dv = v.shape[-1]
    nb = t // BLOCK_Q
    scale = d ** -0.5
    halo = [(0, 0), (BLOCK_Q, BLOCK_Q), (0, 0), (0, 0)]
    kp = jnp.pad(k, halo).reshape(b, nb + 2, BLOCK_Q, hk, d)
    vp = jnp.pad(v, halo).reshape(b, nb + 2, BLOCK_Q, hk, dv)
    kb = jnp.concatenate([kp[:, :-2], kp[:, 1:-1], kp[:, 2:]], axis=2)
    vb = jnp.concatenate([vp[:, :-2], vp[:, 1:-1], vp[:, 2:]], axis=2)
    qb = q.reshape(b, nb, BLOCK_Q, hk, g, d)
    rel_q = jnp.arange(BLOCK_Q)[:, None]
    rel_k = jnp.arange(3 * BLOCK_Q)[None, :] - BLOCK_Q
    abs_k = jnp.arange(nb)[:, None, None] * BLOCK_Q + rel_k[None]
    mask = (jnp.abs(rel_q - rel_k) <= WINDOW)[None] & (abs_k >= 0) & (abs_k < t)
    s_loc = jnp.einsum("bnqhgd,bnkhd->bhgnqk", qb, kb).astype(jnp.float32) * scale
    s_loc = jnp.where(mask[None, None, None], s_loc, NEG_INF)
    s_ctx = jnp.einsum("bnqhgd,bkhd->bhgnqk", qb, k_ctx).astype(jnp.float32) * scale
    s_sink = jnp.broadcast_to(sink.reshape(1, hk, g, 1, 1, 1).astype(jnp.float32), s_loc.shape[:-1] + (1,))
    p = jax.nn.softmax(jnp.concatenate([s_loc, s_ctx, s_sink], axis=-1), axis=-1).astype(v.dtype)
    n_loc = 3 * BLOCK_Q
    n_ctx = k_ctx.shape[1]
    o = (jnp.einsum("bhgnqk,bnkhd->bnqhgd", p[..., :n_loc], vb)
         + jnp.einsum("bhgnqk,bkhd->bnqhgd", p[..., n_loc:n_loc + n_ctx], v_ctx))
    return o.reshape(b, t, hk, g, dv)

def modulation(cond, w_mod, b_mod):
    m = jax.nn.silu(cond) @ w_mod + b_mod
    return jnp.split(m[..., None, :], 6, axis=-1)

def modulate(x, shift, scale):
    return x * (1.0 + scale) + shift

def ab_project(h, w_in, q_norm, w_uq, kv_norm):
    b, t, _ = h.shape
    z = h @ w_in
    cuts = [Q_LORA, Q_LORA + KV_LORA, Q_LORA + KV_LORA + ROPE_A, Q_LORA + KV_LORA + ROPE_A + H_B * HD,
            Q_LORA + KV_LORA + ROPE_A + H_B * HD + KVH_B * HD]
    q_lat, ckv, kpe, qb, kb, vb = jnp.split(z, cuts, axis=-1)
    q_a = (rms_norm(q_lat, q_norm) @ w_uq).reshape(b, t, H_A, NOPE_A + ROPE_A)
    ckv = rms_norm(ckv, kv_norm)
    qb = qb.reshape(b, t, KVH_B, H_B // KVH_B, HD)
    kb = kb.reshape(b, t, KVH_B, HD)
    vb = vb.reshape(b, t, KVH_B, HD)
    return q_a, ckv, kpe, qb, kb, vb

def mla_keys(ckv, kpe, w_ukv):
    b, t, _ = ckv.shape
    kv = (ckv @ w_ukv).reshape(b, t, H_A, NOPE_A + V_A)
    k = jnp.concatenate([kv[..., :NOPE_A], jnp.broadcast_to(kpe[:, :, None, :], (b, t, H_A, ROPE_A))], axis=-1)
    return k, kv[..., NOPE_A:]

def ab_context(h, w_in, q_norm, w_uq, kv_norm, w_ukv, sink, w_out):
    b, t, _ = h.shape
    q_a, ckv, kpe, qb, kb, vb = ab_project(h, w_in, q_norm, w_uq, kv_norm)
    k_a, v_a = mla_keys(ckv, kpe, w_ukv)
    o_a = block_sweep(q_a[:, :, :, None, :], k_a, v_a)
    o_b = block_sweep(qb, kb, vb, sink)
    out = jnp.concatenate([o_a.reshape(b, t, -1), o_b.reshape(b, t, -1)], axis=-1) @ w_out
    return out, ckv, kpe, kb, vb

def ab_latent(h, ckv_ctx, kpe_ctx, kb_ctx, vb_ctx, w_in, q_norm, w_uq, kv_norm, w_ukv, sink, w_out):
    b, t, _ = h.shape
    q_a, ckv, kpe, qb, kb, vb = ab_project(h, w_in, q_norm, w_uq, kv_norm)
    cos_a, sin_a = grid_angles(t, ROPE_A)
    cos_b, sin_b = grid_angles(t, HD)
    q_a = jnp.concatenate([q_a[..., :NOPE_A], apply_rope(q_a[..., NOPE_A:], cos_a, sin_a)], axis=-1)
    kpe = apply_rope(kpe, cos_a, sin_a)
    k_a, v_a = mla_keys(jnp.concatenate([ckv, ckv_ctx], axis=1), jnp.concatenate([kpe, kpe_ctx], axis=1), w_ukv)
    o_a = block_sweep(q_a[:, :, :, None, :], k_a, v_a)
    qb = apply_rope(qb, cos_b, sin_b)
    kb = apply_rope(kb, cos_b, sin_b)
    o_b = band_attend(qb, kb, vb, kb_ctx, vb_ctx, sink)
    return jnp.concatenate([o_a.reshape(b, t, -1), o_b.reshape(b, t, -1)], axis=-1) @ w_out

def c_project(h, w_in, q_norm, k_norm):
    b, t, _ = h.shape
    q, k, v = jnp.split(h @ w_in, [H_C * HD, H_C * HD + KVH_C * HD], axis=-1)
    q = rms_norm(q.reshape(b, t, KVH_C, H_C // KVH_C, HD), q_norm)
    k = rms_norm(k.reshape(b, t, KVH_C, HD), k_norm)
    return q, k, v.reshape(b, t, KVH_C, HD)

def c_context(h, w_in, q_norm, k_norm, w_out):
    b, t, _ = h.shape
    q, k, v = c_project(h, w_in, q_norm, k_norm)
    o = block_sweep(q, k, v)
    return o.reshape(b, t, -1) @ w_out, k, v

def c_latent(h, k_ctx, v_ctx, w_in, q_norm, k_norm, w_out):
    b, t, _ = h.shape
    q, k, v = c_project(h, w_in, q_norm, k_norm)
    cos, sin = grid_angles(t, HD)
    q = apply_rope(q, cos, sin)
    k = apply_rope(k, cos, sin)
    o = block_sweep(q, jnp.concatenate([k, k_ctx], axis=1), jnp.concatenate([v, v_ctx], axis=1))
    return o.reshape(b, t, -1) @ w_out

def moe(h, router_w, router_bias, w_gate, w_up, w_down):
    b, t, d = h.shape
    x = h.reshape(-1, d)
    aff = jax.nn.sigmoid((x @ router_w).astype(jnp.float32))
    sel = aff + router_bias.astype(jnp.float32)
    grp_score = lax.top_k(sel.reshape(-1, N_GROUPS, EXPERTS_PER_GROUP), TOP_K)[0].sum(-1)
    g_idx = jnp.argmax(grp_score, axis=-1)
    in_group = (jnp.arange(N_EXPERTS) // EXPERTS_PER_GROUP)[None, :] == g_idx[:, None]
    _, e_idx = lax.top_k(jnp.where(in_group, sel, -jnp.inf), TOP_K)
    w = jnp.take_along_axis(aff, e_idx, axis=-1)
    w = w / jnp.sum(w, axis=-1, keepdims=True)
    gates = jnp.sum(jax.nn.one_hot(e_idx, N_EXPERTS, dtype=jnp.float32) * w[..., None], axis=1)
    hid = jax.nn.silu(jnp.einsum("nd,edf->nef", x, w_gate)) * jnp.einsum("nd,edf->nef", x, w_up)
    y = jnp.einsum("nef,efd->nd", hid * gates[:, :, None].astype(hid.dtype), w_down)
    return y.reshape(b, t, d)

def setup_inputs(seed: int = 0) -> dict:
    key = jax.random.key(seed)
    ks = iter(jax.random.split(key, 40))

    def nrm(shape, scale):
        return jax.random.normal(next(ks), shape, jnp.float32) * scale

    d = D_MODEL
    return {
        "x_prompt": nrm((BATCH, SEQ, d), 1.0),
        "x_sample": nrm((DEC_BATCH, DEC_SEQ, d), 1.0),
        "c": nrm((DEC_BATCH, d), 1.0),
        "cache_mla_ckv": nrm((DEC_BATCH, N_EVEN, PAST_LEN, KV_LORA), 1.0),
        "cache_mla_kpe": nrm((DEC_BATCH, N_EVEN, PAST_LEN, ROPE_A), 1.0),
        "cache_swa_k": nrm((DEC_BATCH, N_EVEN, PAST_LEN, KVH_B, HD), 1.0),
        "cache_swa_v": nrm((DEC_BATCH, N_EVEN, PAST_LEN, KVH_B, HD), 1.0),
        "cache_gqa_k": nrm((DEC_BATCH, N_ODD, PAST_LEN, KVH_C, HD), 1.0),
        "cache_gqa_v": nrm((DEC_BATCH, N_ODD, PAST_LEN, KVH_C, HD), 1.0),
        "c_ctx": nrm((d,), 1.0),
        "w_mod": nrm((DEPTH, d, 6 * d), 0.5 * d ** -0.5),
        "b_mod": nrm((DEPTH, 6 * d), 0.02),
        "ln_g": 1.0 + nrm((DEPTH, 2, d), 0.02),
        "ln_b": nrm((DEPTH, 2, d), 0.02),
        "w_in_ab": nrm((N_EVEN, d, AB_IN), d ** -0.5),
        "mla_q_norm": 1.0 + nrm((N_EVEN, Q_LORA), 0.02),
        "mla_w_uq": nrm((N_EVEN, Q_LORA, H_A * (NOPE_A + ROPE_A)), Q_LORA ** -0.5),
        "mla_kv_norm": 1.0 + nrm((N_EVEN, KV_LORA), 0.02),
        "mla_w_ukv": nrm((N_EVEN, KV_LORA, H_A * (NOPE_A + V_A)), KV_LORA ** -0.5),
        "swa_sink": nrm((N_EVEN, H_B), 0.5),
        "w_out_ab": nrm((N_EVEN, AB_OUT, d), BETA * AB_OUT ** -0.5),
        "w_in_c": nrm((N_ODD, d, C_IN), d ** -0.5),
        "gqa_q_norm": 1.0 + nrm((N_ODD, HD), 0.02),
        "gqa_k_norm": 1.0 + nrm((N_ODD, HD), 0.02),
        "w_out_c": nrm((N_ODD, C_OUT, d), BETA * C_OUT ** -0.5),
        "router_w": nrm((d, N_EXPERTS), d ** -0.5),
        "router_bias": nrm((N_EXPERTS,), 0.01),
        "exp_w_gate": nrm((DEPTH, N_EXPERTS, d, D_EXPERT), d ** -0.5),
        "exp_w_up": nrm((DEPTH, N_EXPERTS, d, D_EXPERT), d ** -0.5),
        "exp_w_down": nrm((DEPTH, N_EXPERTS, D_EXPERT, d), BETA * D_EXPERT ** -0.5),
    }

def reference(x_prompt, x_sample, c, cache_mla_ckv, cache_mla_kpe, cache_swa_k, cache_swa_v, cache_gqa_k,
              cache_gqa_v, c_ctx, w_mod, b_mod, ln_g, ln_b, w_in_ab, mla_q_norm, mla_w_uq, mla_kv_norm, mla_w_ukv,
              swa_sink, w_out_ab, w_in_c, gqa_q_norm, gqa_k_norm, w_out_c, router_w, router_bias, exp_w_gate,
              exp_w_up, exp_w_down):
    xp = x_prompt
    xs = x_sample
    st_ckv, st_kpe, st_swk, st_swv, st_gk, st_gv = [], [], [], [], [], []
    for l in range(DEPTH):
        i = l // 2
        mp = modulation(c_ctx, w_mod[l], b_mod[l])
        ms = modulation(c, w_mod[l], b_mod[l])
        hp = modulate(xp, mp[0], mp[1])
        hs = modulate(xs, ms[0], ms[1])
        if l % 2 == 0:
            sink = swa_sink[i].reshape(KVH_B, H_B // KVH_B)
            op, ckv, kpe, kb, vb = ab_context(hp, w_in_ab[i], mla_q_norm[i], mla_w_uq[i], mla_kv_norm[i],
                                              mla_w_ukv[i], sink, w_out_ab[i])
            os_ = ab_latent(hs, cache_mla_ckv[:, i], cache_mla_kpe[:, i], cache_swa_k[:, i], cache_swa_v[:, i],
                            w_in_ab[i], mla_q_norm[i], mla_w_uq[i], mla_kv_norm[i], mla_w_ukv[i], sink, w_out_ab[i])
            st_ckv.append(ckv)
            st_kpe.append(kpe)
            st_swk.append(kb)
            st_swv.append(vb)
        else:
            op, kc, vc = c_context(hp, w_in_c[i], gqa_q_norm[i], gqa_k_norm[i], w_out_c[i])
            os_ = c_latent(hs, cache_gqa_k[:, i], cache_gqa_v[:, i], w_in_c[i], gqa_q_norm[i], gqa_k_norm[i],
                           w_out_c[i])
            st_gk.append(kc)
            st_gv.append(vc)
        xp = layer_norm(ALPHA * xp + mp[2] * op, ln_g[l, 0], ln_b[l, 0])
        xs = layer_norm(ALPHA * xs + ms[2] * os_, ln_g[l, 0], ln_b[l, 0])
        hp = modulate(xp, mp[3], mp[4])
        hs = modulate(xs, ms[3], ms[4])
        fp = moe(hp, router_w, router_bias, exp_w_gate[l], exp_w_up[l], exp_w_down[l])
        fs = moe(hs, router_w, router_bias, exp_w_gate[l], exp_w_up[l], exp_w_down[l])
        xp = layer_norm(ALPHA * xp + mp[5] * fp, ln_g[l, 1], ln_b[l, 1])
        xs = layer_norm(ALPHA * xs + ms[5] * fs, ln_g[l, 1], ln_b[l, 1])
    return (xp, xs, jnp.stack(st_ckv, axis=1), jnp.stack(st_kpe, axis=1), jnp.stack(st_swk, axis=1),
            jnp.stack(st_swv, axis=1), jnp.stack(st_gk, axis=1), jnp.stack(st_gv, axis=1))


_drawn_inputs = setup_inputs


def setup_inputs(seed=0):
    import zlib

    import numpy as np

    out = dict(_drawn_inputs(seed))
    spreads = {}
    factors = {'cache_mla_ckv': 7.169,
     'cache_mla_kpe': 7.182,
     'cache_swa_k': 7.294,
     'cache_swa_v': 5.129,
     'cache_gqa_k': 8.0,
     'cache_gqa_v': 6.313,
     'mla_q_norm': 8.0,
     'mla_w_uq': 5.226,
     'mla_kv_norm': 2.863,
     'swa_sink': 58.736,
     'gqa_q_norm': 8.0,
     'gqa_k_norm': 9.102,
     'router_bias': 3.388}
    for name, (base, spread) in spreads.items():
        noise = np.random.default_rng([zlib.crc32(name.encode()), seed]).standard_normal(out[name].shape)
        drawn = base * np.exp(spread * noise) if base else spread * noise
        out[name] = __import__('jax').numpy.asarray(drawn.astype(out[name].dtype))
    for name, factor in factors.items():
        out[name] = (out[name] * factor).astype(out[name].dtype)
    return out
```

```python
from contextlib import ExitStack

import numpy as np

import concourse.bass as bass
from concourse import mybir

F32 = mybir.dt.float32
I32 = mybir.dt.int32
ALU = mybir.AluOpType
ACT = mybir.ActivationFunctionType
AX = mybir.AxisListType

P = 128
G = 2
D = 1024
KD = D // P
DEPTH = 2
GRID_W = 64
ROPE_THETA = 10000.0
EPS = 1e-6
ALPHA = (2 * DEPTH) ** 0.25
HD = 64
Q_LORA, KV_LORA, ROPE_A, NOPE_A = 256, 128, 32, 64
QK_A = NOPE_A + ROPE_A
H_B, KVH_B = 8, 2
H_C, KVH_C = 16, 4
Z_CKV = Q_LORA
Z_KPE = Z_CKV + KV_LORA
Z_QB = Z_KPE + ROPE_A
Z_KB = Z_QB + H_B * HD
Z_VB = Z_KB + KVH_B * HD
AB_IN = Z_VB + KVH_B * HD
Z_KC = H_C * HD
Z_VC = Z_KC + KVH_C * HD
C_IN = Z_VC + KVH_C * HD
N_EXP, N_GRP, PER_GRP, F_EXP = 16, 4, 4, 512
SLOTS = 64
N_CHUNKS = G * P // SLOTS
HALF = 512
BLK = 4096
RING = 9

C_ID, C_TRI, C_ONE, C_SEL, C_BIAS, C_IOTA, C_PRIO, C_LOW, C_COSA, C_SINA, C_COSB, C_SINB = (
    0, 128, 256, 384, 416, 480, 544, 548, 564, 580, 596, 628)
C_COLS = 660
SMALL_LOADS = 8 * 16
N_MOD = 6 * D // HALF
LN_ROW = 32


def shape_constants():
    t = np.zeros((P, C_COLS), np.float32)
    i = np.arange(P)
    t[:, C_ID:C_ID + P] = np.eye(P)
    t[:, C_TRI:C_TRI + P] = i[:, None] < i[None, :]
    t[:, C_ONE:C_ONE + P] = 1.0
    t[:, C_SEL:C_SEL + 32] = (i[:, None] % 32) == np.arange(32)[None, :]
    for l in range(DEPTH):
        for c in range(N_MOD):
            t[l * N_MOD + c, C_BIAS + 32 * l + 2 * c:C_BIAS + 32 * l + 2 * c + 2] = 1.0
    t[:, C_IOTA:C_IOTA + SLOTS] = np.arange(SLOTS)
    t[:, C_PRIO:C_PRIO + N_GRP] = N_GRP - np.arange(N_GRP)
    low = (np.arange(PER_GRP)[None, :] < np.arange(PER_GRP)[:, None])
    t[:, C_LOW:C_LOW + PER_GRP * PER_GRP] = low.reshape(1, -1)
    for width, cc, cs in ((ROPE_A, C_COSA, C_SINA), (HD, C_COSB, C_SINB)):
        n_freq = width // 4
        inv = (1.0 / (ROPE_THETA ** (np.arange(n_freq, dtype=np.float32) / n_freq))).astype(np.float32)
        row, col = (i // GRID_W).astype(np.float32), (i % GRID_W).astype(np.float32)
        ang = np.concatenate([row[:, None] * inv, col[:, None] * inv], axis=-1)
        t[:, cc:cc + width // 2] = np.cos(ang)
        t[:, cs:cs + width // 2] = np.sin(ang)
    return t


def plan_blocks():
    order = [("mod", 0, c) for c in range(4)]
    order += [("win", 0, b) for b in range(3)] + [("lora", 0, 0)] + [("wout", 0, b) for b in range(2)]
    order += [("mod", 0, c) for c in range(4, N_MOD)] + [("mod", 1, c) for c in range(4)]
    order += [("exp", 0, b) for b in range(3 * N_EXP)]
    order += [("win", 1, b) for b in range(4)] + [("wout", 1, b) for b in range(2)]
    order += [("mod", 1, c) for c in range(4, N_MOD)]
    order += [("exp", 1, b) for b in range(3 * N_EXP)]
    return order


WIN = {0: [(0, Z_QB), (Z_QB, Z_KB), (Z_KB, AB_IN)], 1: [(0, 512), (512, 1024), (1024, 1280), (1280, C_IN)]}


def attention_units(layer):
    segments, u = [], 0
    kv_heads = KVH_B if layer == 0 else KVH_C
    seg = []
    for kv in range(kv_heads):
        seg.append((u, "gqa", 0, kv, (0, 1, 2, 3)))
        u += 1
    for kv in range(kv_heads):
        for pair in ((0, 1), (2, 3)):
            seg.append((u, "gqa", 1, kv, pair))
            u += 1
    segments.append((None, seg))
    if layer == 0:
        for g, quad in ((0, 0), (0, 1), (1, 0), (1, 1)):
            seg = []
            for heads in ([(0, 1, 2, 3)] if g == 0 else [(0, 1), (2, 3)]):
                seg.append((u, "mla", g, quad, heads))
                u += 1
            segments.append(((g, quad), seg))
    return segments


def unit_chunks(layer, unit):
    _, kind, g, kv, heads = unit
    base = (4 if layer == 0 else 0) if kind == "gqa" else 0
    return [base + 2 * kv + heads[i] // 2 for i in range(0, len(heads), 2)]


class Turns:

    def __init__(self):
        self.count = [0] * 8
        self.at = {}

    def use(self, key, bank, n=1):
        assert key not in self.at
        self.at[key] = (bank, self.count[bank])
        self.count[bank] += n


def plan_turns():
    t = Turns()
    t.use(("modA", 0), 7)
    for l in range(DEPTH):
        for s in range(2):
            if s == 1:
                t.use(("modB", l), 4)
                for g in range(G):
                    for hf in range(2):
                        t.use(("gate", l, 0, g, hf), 5 + hf)
                for i, key in enumerate([(0, 0), (1, 0), (0, 1), (1, 1)]):
                    t.use(("ln", l, 0) + key, (7, 4, 5, 6)[i])
            for g in range(G):
                for hf in range(2):
                    t.use(("scale", l, s, g, hf), 2 * hf)
                    t.use(("shift", l, s, g, hf), 2 * hf + 1)
            for g in range(G):
                for q in range(2):
                    t.use(("hT", l, s, g, q), 4 + q)
            if s == 0:
                for b in range(len(WIN[l])):
                    for g in range(G):
                        t.use(("z", l, b, g), (2 * b + g) % 4)
                if l == 0:
                    for g in range(G):
                        t.use(("qT", 0, g, 0), 4 + g)
                    t.use(("kT", 0, 0), 6)
                    t.use(("qlatT",), 7)
                    t.use(("ckvT",), 4)
                    t.use(("krT",), 5)
                else:
                    for g in range(G):
                        for j in range(2):
                            t.use(("qT", 1, g, j), 4 + j)
                    for j in range(2):
                        t.use(("kT", 1, j), 6 + j)
                for g in range(G):
                    for hf in range(2):
                        t.use(("y", l, 0, g, hf), 2 * g + hf)
                for group, seg in attention_units(l):
                    if group is not None:
                        g, quad = group
                        t.use(("kn", g, quad, 0), 4)
                        if g == 1:
                            t.use(("kn", g, quad, 1), 5)
                        t.use(("va", g, quad), 6)
                        t.use(("qa", g, quad), 7)
                        t.use(("qaT", g, quad), 4)
                    for unit in seg:
                        u = unit[0]
                        t.use(("S", l, u), 4 + u % 2)
                        t.use(("T", l, u), 6)
                        t.use(("O", l, u), 7)
            else:
                t.use(("logits", l), 6)
                if l == 0:
                    t.use(("modA", 1), 4)
                t.use(("pos", l), 7)
                for g in range(G):
                    for hf in range(2):
                        t.use(("y", l, 1, g, hf), 2 * g + hf)
                t.use(("xe", l), 5, N_EXP)
                t.use(("gu", l), 4, N_EXP)
                t.use(("tp", l), 6, N_EXP)
                t.use(("ye", l), 7, N_EXP)
                for g in range(G):
                    for hf in range(2):
                        t.use(("gate", l, 1, g, hf), 5 + hf)
                for i, key in enumerate([(0, 0), (1, 0), (0, 1), (1, 1)]):
                    t.use(("ln", l, 1) + key, (7, 4, 5, 6)[i])
    return t.at


class Chain:

    def __init__(self, eng, sem):
        self.eng, self.sem, self.n, self.off = eng, sem, 0, 0

    def then(self, ins):
        self.n += 1
        ins.then_inc(self.sem, 1)
        self.eng.wait_ge(self.sem, self.off + self.n)


def hybrid_backbone(nc, i_, o_):
    turn = plan_turns()
    order = plan_blocks()
    index = {}
    for n, b in enumerate(order):
        index.setdefault(b, n)
    lora_n = index[("lora", 0, 0)]

    with ExitStack() as ctx:
        def sb(name, cols, dt=F32):
            return ctx.enter_context(nc.sbuf_tensor(name, [P, cols], dt))

        def sem(name):
            return ctx.enter_context(nc.semaphore(name))

        ring = sb("ring", RING * BLK)
        x = sb("x", G * D)[:].rearrange("p (g d) -> p g d", g=G)
        rows = sb("rows", HALF)
        modA = sb("modA", HALF)
        modB = sb("modB", HALF)
        const = sb("const", C_COLS)
        cwin = sb("cwin", KD * 56)[:].rearrange("p (k w) -> p k w", w=56)
        qn_b = sb("qn_b", Q_LORA)
        kvn_b = sb("kvn_b", KV_LORA)
        sink_b = sb("sink_b", H_B)
        rbias_b = sb("rbias_b", N_EXP)
        cqn_b = sb("cqn_b", HD)
        ckn_b = sb("ckn_b", HD)
        rw = sb("rw", KD * N_EXP)[:].rearrange("p (k e) -> p k e", e=N_EXP)
        cvec = sb("cvec", 2 * KD)[:].rearrange("p (g k) -> p g k", g=G)
        cexp = sb("cexp", 2 * KD)[:].rearrange("p (g k) -> p g k", g=G)
        mhalf = sb("mhalf", 40)
        ss = sb("ss", 40)
        rstd = sb("rstd", 40)
        bnst = sb("bnst", G * 2 * 6)[:].rearrange("p (g h s) -> p g h s", g=G, h=2)
        bnmv = sb("bnmv", G * 2)[:].rearrange("p (g s) -> p g s", g=G)
        lnnb = sb("lnnb", G)
        mx = [sb("mx%d" % b, 4) for b in range(2)]
        negm = [sb("negm%d" % b, 4) for b in range(2)]
        sume = [sb("sume%d" % b, 4) for b in range(2)]
        sinke = [sb("sinke%d" % b, 4) for b in range(2)]
        rsum = [sb("rsum%d" % b, 4) for b in range(2)]
        aff = sb("aff", 32)
        sel = sb("sel", 32)
        pairs = sb("pairs", 48)
        gsc = sb("gsc", 8)
        gmx = sb("gmx", 2)
        gpr = sb("gpr", 8)
        gsel = sb("gsel", 8)
        chosen = sb("chosen", 32)
        wsel = sb("wsel", 32)
        wden = sb("wden", 2)
        pg = sb("pg", 64)[:].rearrange("p (r e) -> p r e", e=N_EXP)
        cur = sb("cur", 4)
        cmax = sb("cmax", 1)
        over = sb("over", 1, I32)
        arena = sb("arena", 10176)

        bank = [ctx.enter_context(nc.psum_tensor(f"bank{b}", [P, HALF], F32)) for b in range(8)]
        filled = [sem(f"filled{b}") for b in range(8)]
        drained = [sem(f"drained{b}") for b in range(8)]
        blk_ready = [sem(f"blk_ready{s}") for s in range(RING)]
        blk_free = sem("blk_free")
        s_load = sem("small_loads")
        s_cache = sem("cache_loads")
        s_zero = sem("rows_zeroed")
        s_rows = sem("rows_loaded")
        s_x = sem("x_loaded")
        s_c = sem("c_loaded")
        s_cexp = sem("cond_exp")
        s_cwin = sem("cond_windows")
        s_dve = sem("dve_order")
        s_pool = sem("pool_order")
        s_pool0 = sem("constants_set")
        s_tick = sem("pool_wait_met")
        s_dve_e = sem("dve_expert_order")
        s_stat = sem("stats_ready")
        s_rstd = sem("rstd_ready")
        s_zfin = sem("z_final")
        s_sq = sem("squares_ready")
        s_qa = sem("qa_ready")
        s_krb = sem("rope_keys_ready")
        s_nm = sem("negmax_ready")
        s_p = sem("probs_ready")
        s_norm = sem("normalised")
        s_lnb = sem("ln_bias_ready")
        s_xnew = sem("x_updated")
        s_affe = sem("affinity_exp")
        s_ch = sem("experts_chosen")
        s_over = sem("overflow_flag")
        s_oh = sem("onehot_ready")
        s_ge = sem("gate_exp_ready")
        s_out = sem("outputs_written")
        ov = [{n: sem(f"ov{l}_{n}") for n in (
            "piece0", "piece1", "used", "oh", "xe", "xeT", "e", "hid", "tp", "hp", "ye", "pool", "dve")}
            for l in range(DEPTH)]

        def cst(c, n, rows_=P):
            return const[0:rows_, c:c + n]

        ident = cst(C_ID, P)
        tri = cst(C_TRI, P)
        ones = cst(C_ONE, P)

        def ar(off, n):
            return arena[:, off:off + n]

        hr = ar(0, G * D).rearrange("p (g d) -> p g d", g=G)
        hT = ar(2048, G * D).rearrange("p (g k t) -> p g k t", g=G, k=KD)
        z = {0: ar(4096, G * AB_IN).rearrange("p (g c) -> p g c", g=G),
             1: ar(4096, G * C_IN).rearrange("p (g c) -> p g c", g=G)}
        rope_cos, rope_sin = ar(1024, 1280), ar(2304, 1280)
        kTa = ar(0, 1024)
        qTa = ar(1024, 512).rearrange("p (h t) -> p h t", h=4)
        va = ar(1536, 512)
        qTc = ar(0, 2048).rearrange("p (g j t) -> p g j t", g=G, j=8)
        prob = [ar(2048 + HALF * b, HALF) for b in range(2)]
        probT = [ar(3072 + HALF * b, HALF) for b in range(2)]
        o0 = 4096 + G * AB_IN
        ckvT, krT = ar(o0, 384), ar(o0 + 384, 384)
        qlatT = ar(o0 + 768, 512).rearrange("p (g c t) -> p g c t", g=G, c=2)
        qbT = ar(o0 + 1280, 1024).rearrange("p (g j t) -> p g j t", g=G, j=4)
        kbT = ar(o0 + 2304, 384)
        cache_vb, cache_kb, cache_c = ar(o0 + 2688, 128), ar(o0 + 2816, 128), ar(o0 + 2944, 160)
        qa = ar(o0 + 2816, 384).rearrange("p (h c) -> p h c", h=4)
        oT_even = [ar(o0 + 3200 + 256 * b, 256) for b in range(2)]
        qa_cos, qa_sin = z[0][:, 0, 0:128], z[0][:, 0, 128:256]
        o1 = 4096 + G * C_IN
        kcT = ar(o1, 768).rearrange("p (j t) -> p j t", j=2)
        cache_kc, cache_vc = ar(o1 + 768, 256), ar(o1 + 1024, 256)
        oT_odd = [ar(o1 + 1280 + 256 * b, 256) for b in range(2)]
        sq = ar(0, 2560).rearrange("p (g h c) -> p g h c", g=G, c=HD)
        rk_gt, rk_eq = ar(2048, 128), ar(2176, 128)
        ov_w = [ar(2048 + 1024 * b, 1024) for b in range(2)]
        xeT = [ar(4096 + HALF * b, HALF) for b in range(3)]
        hp = [ar(5632 + HALF * b, HALF) for b in range(3)]
        ye_sb = ar(7168, HALF)
        e_sb, s_sb, hid, t_sb = (ar(7680 + 256 * i, 256) for i in range(4))
        oh = [ar(8704 + 384 * b, 384).rearrange("p (g c) -> p g c", g=G) for b in range(3)]
        gcopy = [ar(5632 + HALF * b, HALF) for b in range(2)]
        upd = ar(6656, HALF)

        def block_ap(n):
            s = n % RING
            return ring[:, s * BLK:(s + 1) * BLK]

        def got(n, i=None):
            v = 16 * (n // RING + 1) + (16 if n % RING == lora_n % RING and n >= lora_n else 0)
            return blk_ready[n % RING], (v if i is None else i * 16 + v)

        def full(key, e=None):
            b, t = turn[key]
            return filled[b], (t + 1 if e is None else e + (t + 1))

        def saved(key, e=None):
            b, t = turn[key]
            return drained[b], (t + 1 if e is None else e + (t + 1))

        def room(eng, key, e=None):
            b, t = turn[key]
            if e is not None:
                eng.wait_ge(drained[b], e + t)
            elif t > 0:
                eng.wait_ge(drained[b], t)

        def fill(key):
            return filled[turn[key][0]], 1

        def drain(key):
            return drained[turn[key][0]], 1

        def pb(key):
            return bank[turn[key][0]]

        def out_T(l, u):
            return (oT_even if l == 0 else oT_odd)[u % 2]

        w_mod = i_["w_mod"].rearrange("l (p k) c -> l p k c", k=KD)
        w_in = {0: i_["w_in_ab"][0].rearrange("(k p) c -> p k c", p=P),
                1: i_["w_in_c"][0].rearrange("(k p) c -> p k c", p=P)}
        w_out = {0: i_["w_out_ab"][0].rearrange("(k p) c -> p k c", p=P),
                 1: i_["w_out_c"][0].rearrange("(k p) c -> p k c", p=P)}
        w_gate = i_["exp_w_gate"].rearrange("l e (p k) f -> (l e) p (k f)", k=KD)
        w_up = i_["exp_w_up"].rearrange("l e (p k) f -> (l e) p (k f)", k=KD)
        w_down = i_["exp_w_down"].rearrange("l e (k p) c -> (l e) p k c", p=P)
        w_gate_k = i_["exp_w_gate"].rearrange("l e (p k) f -> (l e) k p f", k=KD)
        w_up_k = i_["exp_w_up"].rearrange("l e (p k) f -> (l e) k p f", k=KD)
        w_down_k = i_["exp_w_down"].rearrange("l e (k p) c -> (l e) k p c", p=P)

        uq = block_ap(lora_n)[:, 0:2 * 768].rearrange("p (c n) -> p c n", c=2)
        ukv = block_ap(lora_n)[:, 1536:2560].rearrange("p (h c) -> p h c", h=8)

        exp_n = [index[("exp", l, 0)] for l in range(DEPTH)]
        n_over = (N_CHUNKS - 1) * N_EXP

        block = ctx.enter_context(nc.Block())

        @block.sync
        def _(sp):
            def load_block(n):
                kind, l, b = order[n]
                dst = block_ap(n)
                if n >= RING:
                    sp.wait_ge(blk_free, n - RING + 1)
                if kind == "mod":
                    sp.dma_start(dst.rearrange("p (k c) -> p k c", k=KD),
                                 w_mod[l, :, :, b * HALF:(b + 1) * HALF]).then_inc(got(n)[0], 16)
                elif kind == "win":
                    c0, c1 = WIN[l][b]
                    sp.dma_start(dst[:, 0:KD * (c1 - c0)].rearrange("p (k c) -> p k c", k=KD),
                                 w_in[l][:, :, c0:c1]).then_inc(got(n)[0], 16)
                elif kind == "lora":
                    sp.dma_start(uq, i_["mla_w_uq"][0].rearrange("(c p) n -> p c n", p=P)).then_inc(got(n)[0], 16)
                    sp.dma_start(dst[:, 1536:2560], i_["mla_w_ukv"][0]).then_inc(got(n)[0], 16)
                else:
                    sp.dma_start(dst.rearrange("p (k c) -> p k c", k=4),
                                 w_out[l][:, 4 * b:4 * b + 4, :]).then_inc(got(n)[0], 16)

            def load_expert(l, j, i=None):
                n = exp_n[l] + 3 * j
                e = l * N_EXP + j if i is None else i * 3 + (l * N_EXP + j)
                for t, src in enumerate((w_gate, w_up, w_down)):
                    m = n + t - RING + 1
                    sp.wait_ge(blk_free, m if i is None else i * 9 + m)
                    dst = block_ap(n + t)
                    if t == 2:
                        dst = dst.rearrange("p (k c) -> p k c", k=4)
                    sp.dma_start(dst, src[e]).then_inc(got(n + t)[0], 16)

            def load_experts(l):
                with sp.Fori(0, N_EXP // 3) as i:
                    for j in range(3):
                        load_expert(l, j, i)
                load_expert(l, N_EXP - 1)

            def overflow(l):
                o = ov[l]
                sp.wait_ge(s_over, l + 1)
                most = sp.value_load(over[0:1, 0:1], min_val=0, max_val=G * P)
                with sp.If(most > SLOTS):
                    with sp.Fori(0, N_EXP) as e:
                        with sp.Fori(0, N_CHUNKS - 1) as c:
                            q = (e * (N_CHUNKS - 1) + c) * 12
                            for p in range(12):
                                sp.wait_ge(o["used"], q + (p + 1))
                                if p < 8:
                                    a, b = w_gate_k[e + l * N_EXP, p], w_up_k[e + l * N_EXP, p]
                                else:
                                    a = w_down_k[e + l * N_EXP, p - 8, :, 0:HALF]
                                    b = w_down_k[e + l * N_EXP, p - 8, :, HALF:D]
                                sp.dma_start(ov_w[p % 2][:, 0:HALF], a).then_inc(o[f"piece{p % 2}"], 16)
                                sp.dma_start(ov_w[p % 2][:, HALF:D], b).then_inc(o[f"piece{p % 2}"], 16)

            for n in range(exp_n[0]):
                load_block(n)
            load_experts(0)
            overflow(0)
            for n in range(exp_n[0] + 3 * N_EXP, exp_n[1]):
                load_block(n)
            load_experts(1)
            overflow(1)
            sp.wait_ge(s_xnew, 4 * DEPTH)
            sp.dma_start(o_["y_prompt"][0], x[:, 0, :]).then_inc(s_out, 16)
            for hf in range(2):
                sp.wait_ge(*saved(("ln", DEPTH - 1, 1, 1, hf)))
            sp.dma_start(o_["y_sample"][0], x[:, 1, :]).then_inc(s_out, 16)
            sp.wait_ge(s_out, 16 * 8)

        @block.tensor
        def _(pe):
            def bcast(key, lhs_col, rhs):
                room(pe, key)
                nc.tensor.matmul(pb(key)[:], lhs_col.to_broadcast([P, P]), rhs,
                                 start=True, stop=True).then_inc(*fill(key))

            def mod_row(key, part, g, hf):
                src = modA if part < 2 else modB
                bcast(key, cst(C_SEL + 2 * (2 * part + hf) + g, 1), src[:])

            def ln_row(key, l, s, which, hf):
                bcast(key, cst(C_ID + LN_ROW + 8 * which + 2 * (2 * l + s) + hf, 1), rows[:])

            def modulation(l, name, free=0):
                key = (name, l)
                room(pe, key)
                chunks = range(4) if name == "modA" else range(4, N_MOD)
                out = pb(key)
                for c in chunks:
                    n = index[("mod", l, c)]
                    pe.wait_ge(*got(n))
                    w = block_ap(n)
                    for k in range(KD):
                        j = k % 4
                        mm = nc.tensor.matmul(out[32 * j:32 * j + 32, :], cwin[:, k, 24 - 2 * c:56 - 2 * c],
                                              w[:, k * HALF:(k + 1) * HALF],
                                              start=(c == chunks[0] and k < 4), stop=False, skip_group_check=True)
                        if free and c == chunks[0] and k == 0:
                            mm.then_inc(blk_free, free)
                    mm.then_inc(blk_free, 1)
                nc.tensor.matmul(out[0:32, :], cst(C_BIAS + 32 * l, 32, DEPTH * N_MOD), rows[0:DEPTH * N_MOD, :],
                                 start=False, stop=True, skip_group_check=True).then_inc(*fill(key))

            def modulated(l, s):
                def pair(g, hf):
                    mod_row(("scale", l, s, g, hf), 3 * s + 1, g, hf)
                    mod_row(("shift", l, s, g, hf), 3 * s, g, hf)

                def turned(g, q):
                    key = ("hT", l, s, g, q)
                    room(pe, key)
                    pe.wait_ge(*saved(("shift", l, s, g, q)))
                    for k in range(4):
                        mm = nc.tensor.transpose(pb(key)[:, k * P:(k + 1) * P],
                                                 hr[:, g, (4 * q + k) * P:(4 * q + k + 1) * P], ident)
                        if (l, s, g, q, k) == (1, 0, 0, 0, 0):
                            mm.then_inc(blk_free, 1)
                    mm.then_inc(*fill(key))

                pair(0, 0)
                pair(0, 1)
                turned(0, 0)
                pair(1, 0)
                turned(0, 1)
                pair(1, 1)
                turned(1, 0)
                turned(1, 1)

            def project(l):
                for b, (c0, c1) in enumerate(WIN[l]):
                    n = index[("win", l, b)]
                    pe.wait_ge(*got(n))
                    w = block_ap(n)[:, 0:KD * (c1 - c0)].rearrange("p (k c) -> p k c", k=KD)
                    for g in range(G):
                        key = ("z", l, b, g)
                        room(pe, key)
                        if b == 0:
                            pe.wait_ge(*saved(("hT", l, 0, g, 1)))
                            pe.wait_ge(*saved(("hT", l, 0, g, 0)))
                        for k in range(KD):
                            mm = nc.tensor.matmul(pb(key)[:, 0:c1 - c0], hT[:, g, k, :], w[:, k, :],
                                                  start=(k == 0), stop=(k == KD - 1))
                        mm.then_inc(*fill(key))

            def transposes(key, ins, width=P, free=0):
                room(pe, key)
                for j, a in enumerate(ins):
                    mm = nc.tensor.transpose(pb(key)[0:width, j * P:(j + 1) * P], a, ident)
                    if j == 0 and free:
                        mm.then_inc(blk_free, free)
                mm.then_inc(*fill(key))

            def scores(l, unit):
                u, kind, g, kv, heads = unit
                key = ("S", l, u)
                room(pe, key)
                nk = P if g == 0 else 2 * P
                k0 = 0 if g == 0 else P
                if kind == "mla" and heads[0] == 0:
                    pe.wait_ge(s_krb, 2 * g + kv + 1)
                    for b in range(1 + g):
                        pe.wait_ge(*saved(("kn", g, kv, b)))
                    pe.wait_ge(*saved(("qaT", g, kv)))
                for i, h in enumerate(heads):
                    if kind == "mla":
                        lhs = qTa[0:QK_A, h, :]
                        rhs = kTa[0:QK_A, h * nk:(h + 1) * nk]
                    else:
                        r = HD * (kv % 2)
                        if l == 0:
                            lhs, rhs = qbT[r:r + HD, g, h, :], kbT[r:r + HD, k0:k0 + nk]
                        else:
                            lhs = qTc[r:r + HD, g, 4 * (kv // 2) + h, :]
                            rhs = kcT[r:r + HD, kv // 2, k0:k0 + nk]
                    mm = nc.tensor.matmul(pb(key)[:, i * nk:(i + 1) * nk], lhs, rhs, start=True, stop=True)
                mm.then_inc(*fill(key))

            def turn_probs(l, unit):
                u = unit[0]
                key = ("T", l, u)
                room(pe, key)
                pe.wait_ge(s_p, u + 1 + 12 * l)
                for j in range(4):
                    mm = nc.tensor.transpose(pb(key)[:, j * P:(j + 1) * P], prob[u % 2][:, j * P:(j + 1) * P], ident)
                mm.then_inc(*fill(key))

            def values(l, unit):
                u, kind, g, kv, heads = unit
                key = ("O", l, u)
                room(pe, key)
                pe.wait_ge(*saved(("T", l, u)))
                if kind == "mla":
                    pe.wait_ge(*saved(("va", g, kv)))
                nkt = 1 if g == 0 else 2
                for i, h in enumerate(heads):
                    half = HD * (h % 2)
                    for kt in range(nkt):
                        if kind == "mla":
                            v = va[:, kt * 256 + h * HD:kt * 256 + (h + 1) * HD]
                        elif l == 0:
                            v = z[0][:, g, Z_VB + kv * HD:Z_VB + (kv + 1) * HD] if kt == 0 else \
                                cache_vb[:, kv * HD:(kv + 1) * HD]
                        else:
                            v = z[1][:, g, Z_VC + kv * HD:Z_VC + (kv + 1) * HD] if kt == 0 else \
                                cache_vc[:, kv * HD:(kv + 1) * HD]
                        mm = nc.tensor.matmul(pb(key)[half:half + HD, (i // 2) * P:(i // 2 + 1) * P], v,
                                              probT[u % 2][:, (i * nkt + kt) * P:(i * nkt + kt + 1) * P],
                                              start=(kt == 0), stop=(kt == nkt - 1))
                mm.then_inc(*fill(key))

            begun = {}

            def out_project(l, unit):
                u, _, g, _, _ = unit
                pe.wait_ge(*saved(("O", l, u)))
                for ci, c in enumerate(unit_chunks(l, unit)):
                    n = index[("wout", l, c // 4)]
                    pe.wait_ge(*got(n))
                    w = block_ap(n)
                    first = (l, g) not in begun
                    begun[(l, g)] = begun.get((l, g), 0) + 1
                    for hf in range(2):
                        key = ("y", l, 0, g, hf)
                        if first:
                            room(pe, key)
                        mm = nc.tensor.matmul(pb(key)[:], out_T(l, u)[:, ci * P:(ci + 1) * P],
                                              w[:, (c % 4) * D + hf * HALF:(c % 4) * D + (hf + 1) * HALF],
                                              start=first, stop=(begun[(l, g)] == KD), skip_group_check=True)
                        if begun[(l, g)] == KD:
                            mm.then_inc(*fill(key))

            def mla_group(g, quad):
                nkt = 1 + g
                k0 = P * g
                per = 4 // nkt
                pe.wait_ge(*got(lora_n))
                for h in range(4):
                    key = ("kn", g, quad, h // per)
                    if h % per == 0:
                        room(pe, key)
                    mm = nc.tensor.matmul(pb(key)[0:NOPE_A, (h % per) * nkt * P:(h % per + 1) * nkt * P],
                                          ukv[:, 4 * quad + h, 0:NOPE_A], ckvT[:, k0:k0 + nkt * P],
                                          start=True, stop=True)
                    if h % per == per - 1:
                        mm.then_inc(*fill(key))
                key = ("qa", g, quad)
                room(pe, key)
                for c in range(2):
                    mm = nc.tensor.matmul(pb(key)[:, 0:4 * QK_A], qlatT[:, g, c, :],
                                          uq[:, c, 4 * quad * QK_A:4 * (quad + 1) * QK_A],
                                          start=(c == 0), stop=(c == 1))
                mm.then_inc(*fill(key))
                key = ("va", g, quad)
                room(pe, key)
                for kt in range(nkt):
                    mm = nc.tensor.matmul(pb(key)[:, kt * 256:(kt + 1) * 256], ckvT[:, k0 + kt * P:k0 + (kt + 1) * P],
                                          ukv[:, 4 * quad:4 * quad + 4, NOPE_A:NOPE_A + HD], start=True, stop=True)
                mm.then_inc(*fill(key))
                pe.wait_ge(*saved(("qa", g, quad)))
                if g == 1:
                    pe.wait_ge(s_qa, quad + 1)
                transposes(("qaT", g, quad), [qa[:, h, :] for h in range(4)], width=QK_A)

            def attention(l):
                if l == 0:
                    pe.wait_ge(*saved(("z", 0, 2, 0)))
                    pe.wait_ge(*saved(("z", 0, 1, 0)))
                    for g in range(G):
                        if g == 1:
                            pe.wait_ge(s_zfin, 1)
                        transposes(("qT", 0, g, 0), [z[0][:, g, Z_QB + j * P:Z_QB + (j + 1) * P] for j in range(4)],
                                   free=len(WIN[0]) if g == 0 else 0)
                    pe.wait_ge(s_cache, 64)
                    transposes(("kT", 0, 0), [z[0][:, 0, Z_KB:Z_VB], z[0][:, 1, Z_KB:Z_VB], cache_kb])
                    pe.wait_ge(s_zfin, 2)
                    transposes(("qlatT",), [z[0][:, g, c * P:(c + 1) * P] for g in range(G) for c in range(2)])
                    transposes(("ckvT",), [z[0][:, 0, Z_CKV:Z_KPE], z[0][:, 1, Z_CKV:Z_KPE], cache_c[:, 0:KV_LORA]])
                    transposes(("krT",), [z[0][:, 0, Z_KPE - NOPE_A:Z_QB], z[0][:, 1, Z_KPE - NOPE_A:Z_QB],
                                          cache_c[:, KV_LORA - NOPE_A:KV_LORA + ROPE_A]], width=QK_A)
                    pe.wait_ge(*saved(("qT", 0, 0, 0)))
                    pe.wait_ge(*saved(("qT", 0, 1, 0)))
                    pe.wait_ge(*saved(("kT", 0, 0)))
                else:
                    for g in range(G):
                        pe.wait_ge(s_zfin, 3 + g)
                        for a in range(2):
                            transposes(("qT", 1, g, a), [z[1][:, g, (4 * a + j) * P:(4 * a + j + 1) * P]
                                                          for j in range(4)],
                                       free=len(WIN[1]) if g == 0 and a == 0 else 0)
                    pe.wait_ge(s_cache, 96)
                    for a in range(2):
                        c = slice(Z_KC + a * P, Z_KC + (a + 1) * P)
                        transposes(("kT", 1, a), [z[1][:, 0, c], z[1][:, 1, c], cache_kc[:, a * P:(a + 1) * P]])
                    for a in range(2):
                        pe.wait_ge(*saved(("qT", 1, 0, a)))
                        pe.wait_ge(*saved(("qT", 1, 1, a)))
                        pe.wait_ge(*saved(("kT", 1, a)))
                for group, seg in attention_units(l):
                    if group is not None:
                        mla_group(*group)
                    for unit in seg[:2]:
                        scores(l, unit)
                    for i, unit in enumerate(seg):
                        turn_probs(l, unit)
                        if i > 0:
                            out_project(l, seg[i - 1])
                        values(l, unit)
                        if i + 2 < len(seg):
                            scores(l, seg[i + 2])
                    out_project(l, seg[-1])

            def ln_rows(l, s):
                for g in range(G):
                    for hf in range(2):
                        mod_row(("gate", l, s, g, hf), 3 * s + 2, g, hf)
                for hf in range(2):
                    ln_row(("ln", l, s, 0, hf), l, s, 0, hf)
                    ln_row(("ln", l, s, 1, hf), l, s, 1, hf)

            def route(l):
                key = ("logits", l)
                room(pe, key)
                for g in range(G):
                    pe.wait_ge(*saved(("hT", l, 1, g, 0)))
                    pe.wait_ge(*saved(("hT", l, 1, g, 1)))
                    for k in range(KD):
                        mm = nc.tensor.matmul(pb(key)[:, g * N_EXP:(g + 1) * N_EXP], hT[:, g, k, :], rw[:, k, :],
                                              start=(g == 0 and k == 0), stop=(k == KD - 1), skip_group_check=True)
                mm.then_inc(*fill(key))
                if l == 0:
                    modulation(1, "modA")
                key = ("pos", l)
                room(pe, key)
                pe.wait_ge(s_ch, l + 1)
                out = pb(key)
                nc.tensor.matmul(out[:, 0:32], tri, chosen[:], start=True, stop=False, skip_group_check=True)
                nc.tensor.matmul(out[:, 16:32], ones, chosen[:, 0:16], start=False, stop=True, skip_group_check=True)
                nc.tensor.matmul(out[:, 64:80], ones, chosen[:, 0:16], start=False, stop=False, skip_group_check=True)
                nc.tensor.matmul(out[:, 64:80], ones, chosen[:, 16:32], start=False, stop=True,
                                 skip_group_check=True).then_inc(*fill(key))

            def gather(out, onehot):
                for k in range(KD):
                    for g in range(G):
                        h = hr[:, g, :].rearrange("p (m k) -> p k m", k=KD)[:, k, :]
                        mm = nc.tensor.matmul(out[:, k * SLOTS:(k + 1) * SLOTS], h, onehot[:, g, 0:SLOTS],
                                              start=(g == 0), stop=(g == 1))
                return mm

            def turn_hidden(out, onehot):
                for c in range(2):
                    yield nc.tensor.transpose(out[:, c * P:(c + 1) * P], hid[:, c * P:(c + 1) * P], ident)
                for g in range(G):
                    yield nc.tensor.transpose(out[:, 256 + g * P:256 + (g + 1) * P], onehot[:, g, SLOTS:3 * SLOTS],
                                              ident)

            def spread(l, buf, first, last):
                for g in range(G):
                    for hf in range(2):
                        r = SLOTS * hf
                        yield nc.tensor.matmul(pb(("y", l, 1, g, hf))[:],
                                               buf[r:r + SLOTS, 256 + g * P:256 + (g + 1) * P],
                                               ye_sb[r:r + SLOTS, :], start=first, stop=last, skip_group_check=True)

            def expert(l, j, i=None, gather_next=True):
                e = j if i is None else i * 3 + j
                n = exp_n[l] + 3 * j
                ring_i = None if i is None else i
                b = j % 3
                room(pe, ("gu", l), e)
                pe.wait_ge(*saved(("xe", l), e))
                pe.wait_ge(*got(n, ring_i))
                pe.wait_ge(*got(n + 1, ring_i))
                s0 = n % RING
                w = ring[:, s0 * BLK:(s0 + 2) * BLK].rearrange("p (w k f) -> p w k f", w=2, k=KD)
                for k in range(KD):
                    for hf in range(2):
                        mm = nc.tensor.matmul(pb(("gu", l))[SLOTS * hf:SLOTS * (hf + 1), :],
                                              xeT[b][:, k * SLOTS:(k + 1) * SLOTS],
                                              w[:, :, k, hf * 256:(hf + 1) * 256], start=(k == 0), stop=(k == KD - 1))
                mm.then_inc(*fill(("gu", l)))
                if gather_next:
                    room(pe, ("xe", l), e + 1)
                    pe.wait_ge(s_oh, e + (N_EXP * l + 2))
                    gather(pb(("xe", l)), oh[(j + 1) % 3]).then_inc(*fill(("xe", l)))
                room(pe, ("tp", l), e)
                pe.wait_ge(*saved(("gu", l), e))
                for q, mm in enumerate(turn_hidden(pb(("tp", l)), oh[b])):
                    if q == 0 and not (i is None and j == 0):
                        mm.then_inc(blk_free, 1)
                    if q == 1:
                        mm.then_inc(blk_free, 2)
                    if q == 3:
                        mm.then_inc(*fill(("tp", l)))
                if not (i is None and j == 0):
                    pe.wait_ge(*saved(("ye", l), e - 1))
                    for mm in spread(l, hp[(j - 1) % 3], i is None and j == 1, False):
                        pass
                else:
                    for g in range(G):
                        for hf in range(2):
                            room(pe, ("y", l, 1, g, hf))
                room(pe, ("ye", l), e)
                pe.wait_ge(*saved(("tp", l), e))
                pe.wait_ge(*got(n + 2, ring_i))
                w = block_ap(n + 2)
                for kf in range(4):
                    lhs = hp[b][:, (kf % 2) * P + (kf // 2) * SLOTS:(kf % 2) * P + (kf // 2 + 1) * SLOTS]
                    for hf in range(2):
                        mm = nc.tensor.matmul(pb(("ye", l))[SLOTS * hf:SLOTS * (hf + 1), :], lhs,
                                              w[:, kf * D + hf * HALF:kf * D + (hf + 1) * HALF],
                                              start=(kf == 0), stop=(kf == 3))
                mm.then_inc(*fill(("ye", l)))

            def experts(l):
                room(pe, ("xe", l), 0)
                pe.wait_ge(s_oh, N_EXP * l + 1)
                gather(pb(("xe", l)), oh[0]).then_inc(*fill(("xe", l)))
                expert(l, 0)
                expert(l, 1)
                with pe.Fori(0, 4) as i:
                    for j in range(2, 5):
                        expert(l, j, i)
                expert(l, 14)
                expert(l, 15, gather_next=False)
                pe.wait_ge(*saved(("ye", l), N_EXP - 1))
                for q, mm in enumerate(spread(l, hp[(N_EXP - 1) % 3], False, True)):
                    mm.then_inc(*fill(("y", l, 1, q // 2, q % 2)))

            def overflow(l):
                o = ov[l]
                pe.wait_ge(s_over, l + 1)
                most = pe.value_load(over[0:1, 0:1], min_val=0, max_val=G * P)
                with pe.If(most > SLOTS):
                    pe.sem_inc(o["used"], 2)
                    with pe.Fori(0, N_EXP) as e:
                        with pe.Fori(0, N_CHUNKS - 1) as c:
                            s = e * (N_CHUNKS - 1) + c
                            pe.wait_ge(o["oh"], s + 1)
                            gather(bank[5], oh[0]).then_inc(o["xe"], 1)
                            pe.wait_ge(o["xeT"], s + 1)
                            for p in range(12):
                                if p == 8:
                                    pe.wait_ge(o["hid"], s + 1)
                                    for q, mm in enumerate(turn_hidden(bank[6], oh[0])):
                                        if q == 3:
                                            mm.then_inc(o["tp"], 1)
                                    pe.wait_ge(o["hp"], s + 1)
                                pe.wait_ge(o[f"piece{p % 2}"], s * 192 + (32 * (p // 2) + 32))
                                w = ov_w[p % 2]
                                for hf in range(2):
                                    if p < 8:
                                        mm = nc.tensor.matmul(
                                            bank[4][SLOTS * hf:SLOTS * (hf + 1), :],
                                            xeT[0][:, p * SLOTS:(p + 1) * SLOTS],
                                            w.rearrange("p (w f) -> p w f", w=2)[:, :, hf * 256:(hf + 1) * 256],
                                            start=(p == 0), stop=(p == 7))
                                    else:
                                        kf = p - 8
                                        lhs = hp[0][:, (kf % 2) * P + (kf // 2) * SLOTS:
                                                    (kf % 2) * P + (kf // 2 + 1) * SLOTS]
                                        mm = nc.tensor.matmul(bank[7][SLOTS * hf:SLOTS * (hf + 1), :], lhs,
                                                              w[:, hf * HALF:(hf + 1) * HALF],
                                                              start=(kf == 0), stop=(kf == 3))
                                mm.then_inc(o["used"], 1)
                            pe.wait_ge(o["ye"], s + 1)
                            for mm in spread(l, hp[0], False, True):
                                pass

            for l in range(DEPTH):
                if l == 0:
                    pe.wait_ge(s_cwin, 1)
                    pe.wait_ge(s_rows, 48)
                    pe.wait_ge(s_load, SMALL_LOADS)
                    modulation(0, "modA")
                pe.wait_ge(*saved(("modA", l)))
                modulated(l, 0)
                project(l)
                attention(l)
                modulation(l, "modB", free=3 if l == 0 else 2)
                pe.wait_ge(*saved(("modB", l)))
                ln_rows(l, 0)
                modulated(l, 1)
                route(l)
                experts(l)
                overflow(l)
                ln_rows(l, 1)

        @block.vector
        def _(dve):
            ch = Chain(dve, s_dve)
            V = nc.vector

            def modulated(l, s):
                for g in range(G):
                    for hf in range(2):
                        cols = slice(hf * HALF, (hf + 1) * HALF)
                        k_scale, k_shift = ("scale", l, s, g, hf), ("shift", l, s, g, hf)
                        dve.wait_ge(*full(k_scale))
                        V.scalar_tensor_tensor(out=hr[:, g, cols], in0=pb(k_scale)[:], scalar=1.0, in1=x[:, g, cols],
                                               op0=ALU.add, op1=ALU.mult).then_inc(*drain(k_scale))
                        dve.wait_ge(*saved(k_scale))
                        dve.wait_ge(*full(k_shift))
                        V.tensor_tensor(hr[:, g, cols], hr[:, g, cols], pb(k_shift)[:],
                                        ALU.add).then_inc(*drain(k_shift))

            def rotate(v, cos, sin, tc, ts):
                n, half = v.shape[1], v.shape[3]
                tc = tc[:, 0:2 * n * half].rearrange("p (n a c) -> p n a c", n=n, a=2)
                ts = ts[:, 0:2 * n * half].rearrange("p (n a c) -> p n a c", n=n, a=2)
                for a in range(2):
                    V.tensor_tensor(tc[:, :, a], v[:, :, a], cos.unsqueeze(1).to_broadcast([P, n, half]), ALU.mult)
                    last = V.tensor_tensor(ts[:, :, a], v[:, :, a], sin.unsqueeze(1).to_broadcast([P, n, half]),
                                           ALU.mult)
                ch.then(last)
                ch.then(V.tensor_tensor(v[:, :, 0], tc[:, :, 0], ts[:, :, 1], ALU.subtract))
                return V.tensor_tensor(v[:, :, 1], tc[:, :, 1], ts[:, :, 0], ALU.add)

            def halves(v, n):
                return v.rearrange("p (n a c) -> p n a c", n=n, a=2)

            def normalise_even():
                for b in range(3):
                    for g in range(G):
                        dve.wait_ge(*saved(("z", 0, b, g)))
                zz = z[0]
                rotate(halves(zz[:, 1, Z_QB:Z_VB], H_B + KVH_B), cst(C_COSB, 32), cst(C_SINB, 32),
                       rope_cos, rope_sin).then_inc(s_zfin, 1)
                for g in range(G):
                    for i, (c0, c1) in enumerate(((0, Z_CKV), (Z_CKV, Z_KPE))):
                        ch.then(V.tensor_tensor_reduce(hr[:, 0, 0:c1 - c0], zz[:, g, c0:c1], zz[:, g, c0:c1], 1.0, 0.0,
                                                       ALU.mult, ALU.add, ss[:, 2 * g + i:2 * g + i + 1]))
                sv = ss[:, 0:4].rearrange("p (g i) -> p i g", i=2)
                ch.then(V.tensor_scalar(sv[:, 0], sv[:, 0], 1.0 / Q_LORA, EPS, ALU.mult, ALU.add))
                V.tensor_scalar(sv[:, 1], sv[:, 1], 1.0 / KV_LORA, EPS, ALU.mult, ALU.add).then_inc(s_stat, 1)
                ch.then(rotate(halves(zz[:, 1, Z_KPE:Z_QB], 1), cst(C_COSA, 16), cst(C_SINA, 16),
                               rope_cos, rope_sin))
                dve.wait_ge(s_rstd, 1)
                for g in range(G):
                    for i, (c0, c1, w) in enumerate(((0, Z_CKV, qn_b), (Z_CKV, Z_KPE, kvn_b))):
                        ins = V.scalar_tensor_tensor(out=zz[:, g, c0:c1], in0=zz[:, g, c0:c1],
                                                     scalar=rstd[:, 2 * g + i:2 * g + i + 1], in1=w[:],
                                                     op0=ALU.mult, op1=ALU.mult)
                        if (g, i) == (1, 1):
                            ins.then_inc(s_zfin, 1)
                        else:
                            ch.then(ins)
                for key, dst in ((("kT", 0, 0), kbT), (("qlatT",), qlatT.rearrange("p g c t -> p (g c t)")),
                                 (("ckvT",), ckvT)):
                    dve.wait_ge(*full(key))
                    V.tensor_copy(dst, pb(key)[:, 0:dst.shape[1]]).then_inc(*drain(key))

            def normalise_odd():
                zz, n = z[1], H_C + KVH_C
                for g in range(G):
                    dve.wait_ge(s_sq, g + 1)
                    ch.then(V.tensor_reduce(ss[:, n * g:n * (g + 1)], sq[:, g], AX.X, ALU.add))
                V.tensor_scalar(ss[:, 0:2 * n], ss[:, 0:2 * n], 1.0 / HD, EPS, ALU.mult, ALU.add).then_inc(s_stat, 1)
                dve.wait_ge(s_rstd, 4)
                for g in range(G):
                    v = zz[:, g, 0:Z_VC].rearrange("p (h c) -> p h c", c=HD)
                    ch.then(V.tensor_tensor(v, v, rstd[:, n * g:n * (g + 1)].unsqueeze(2).to_broadcast([P, n, HD]),
                                            ALU.mult))
                    ch.then(V.tensor_tensor(v[:, 0:H_C], v[:, 0:H_C],
                                            cqn_b[:].unsqueeze(1).to_broadcast([P, H_C, HD]), ALU.mult))
                    ins = V.tensor_tensor(v[:, H_C:n], v[:, H_C:n],
                                          ckn_b[:].unsqueeze(1).to_broadcast([P, KVH_C, HD]), ALU.mult)
                    if g == 0:
                        ins.then_inc(s_zfin, 1)
                    else:
                        ch.then(ins)
                        rotate(halves(zz[:, 1, 0:Z_VC], n), cst(C_COSB, 32), cst(C_SINB, 32),
                               rope_cos, rope_sin).then_inc(s_zfin, 1)
                for a in range(2):
                    dve.wait_ge(*full(("kT", 1, a)))
                    V.tensor_copy(kcT[:, a, :], pb(("kT", 1, a))[:, 0:384]).then_inc(*drain(("kT", 1, a)))

            def unit_max(l, unit):
                u, kind, g, kv, heads = unit
                b, nh = u % 2, len(heads)
                scale = (QK_A if kind == "mla" else HD) ** -0.5
                dve.wait_ge(*full(("S", l, u)))
                ch.then(V.tensor_reduce(mx[b][:, 0:nh], pb(("S", l, u))[:].rearrange("p (h k) -> p h k", h=nh),
                                        AX.X, ALU.max))
                if l == 0 and kind == "gqa":
                    snk = sink_b[:, 4 * kv + heads[0]:4 * kv + heads[0] + nh]
                    ch.then(V.scalar_tensor_tensor(out=mx[b][:, 0:nh], in0=mx[b][:, 0:nh], scalar=scale, in1=snk,
                                                   op0=ALU.mult, op1=ALU.max))
                    ch.then(V.tensor_scalar(negm[b][:, 0:nh], mx[b][:, 0:nh], -1.0, None, ALU.mult))
                    V.tensor_tensor(sinke[b][:, 0:nh], snk, negm[b][:, 0:nh], ALU.add).then_inc(s_nm, 1)
                else:
                    V.tensor_scalar(negm[b][:, 0:nh], mx[b][:, 0:nh], -scale, None, ALU.mult).then_inc(s_nm, 1)

            def unit_normalise(l, unit):
                u, kind, g, kv, heads = unit
                b, nh = u % 2, len(heads)
                dve.wait_ge(*saved(("S", l, u)))
                if l == 0 and kind == "gqa":
                    ch.then(V.tensor_tensor(sume[b][:, 0:nh], sume[b][:, 0:nh], sinke[b][:, 0:nh], ALU.add))
                ch.then(V.reciprocal(rsum[b][:, 0:nh], sume[b][:, 0:nh]))
                pv = prob[b].rearrange("p (h k) -> p h k", h=nh)
                V.tensor_tensor(pv, pv, rsum[b][:, 0:nh].unsqueeze(2).to_broadcast([P, nh, HALF // nh]),
                                ALU.mult).then_inc(s_p, 1)
                dve.wait_ge(*full(("T", l, u)))
                V.tensor_copy(probT[b], pb(("T", l, u))[:]).then_inc(*drain(("T", l, u)))

            def attention(l):
                for group, seg in attention_units(l):
                    if group is not None:
                        g, quad = group
                        dve.wait_ge(*full(("qa", g, quad)))
                        V.tensor_copy(qa.rearrange("p h c -> p (h c)"),
                                      pb(("qa", g, quad))[:, 0:4 * QK_A]).then_inc(*drain(("qa", g, quad)))
                        if g == 1:
                            dve.wait_ge(*saved(("qa", g, quad)))
                            v = qa[:, :, NOPE_A:QK_A].rearrange("p h (a c) -> p h a c", a=2)
                            rotate(v, cst(C_COSA, 16), cst(C_SINA, 16), qa_cos, qa_sin).then_inc(s_qa, 1)
                        n = 256 * (1 + g)
                        dve.wait_ge(*full(("va", g, quad)))
                        V.tensor_copy(va[:, 0:n], pb(("va", g, quad))[:, 0:n]).then_inc(*drain(("va", g, quad)))
                    unit_max(l, seg[0])
                    for i, unit in enumerate(seg):
                        if i + 1 < len(seg):
                            unit_max(l, seg[i + 1])
                        unit_normalise(l, unit)

            def layer_norm(l, s):
                for g in range(G):
                    for hf in range(2):
                        cols = slice(hf * HALF, (hf + 1) * HALF)
                        key = ("y", l, s, g, hf)
                        dve.wait_ge(*full(key))
                        dve.wait_ge(*saved(("gate", l, s, g, hf)))
                        V.tensor_tensor(upd, pb(key)[:], gcopy[hf], ALU.mult).then_inc(*drain(key))
                        dve.wait_ge(*saved(key))
                        ch.then(V.scalar_tensor_tensor(out=x[:, g, cols], in0=x[:, g, cols], scalar=ALPHA, in1=upd,
                                                       op0=ALU.mult, op1=ALU.add))
                        last = V.bn_stats(bnst[:, g, hf, :], x[:, g, cols])
                    ch.then(last)
                    ch.then(V.bn_aggr(bnmv[:, g, :], bnst[:, g].rearrange("p h s -> p (h s)")))
                V.tensor_scalar(ss[:, 0:2], bnmv[:, :, 1], EPS, None, ALU.add).then_inc(s_stat, 1)
                n = (2, 3, 5, 6)[2 * l + s]
                dve.wait_ge(s_rstd, n)
                V.scalar_tensor_tensor(out=lnnb[:], in0=bnmv[:, :, 0], scalar=-1.0, in1=rstd[:, 0:2],
                                       op0=ALU.mult, op1=ALU.mult).then_inc(s_lnb, 1)
                for hf in range(2):
                    cols = slice(hf * HALF, (hf + 1) * HALF)
                    kw, kb = ("ln", l, s, 0, hf), ("ln", l, s, 1, hf)
                    for g in range(G):
                        dve.wait_ge(s_norm, 2 * (2 * l + s) + g + 1)
                        if g == 0:
                            dve.wait_ge(*full(kw))
                            ch.then(V.tensor_tensor(x[:, g, cols], x[:, g, cols], pb(kw)[:], ALU.mult))
                            dve.wait_ge(*full(kb))
                            V.tensor_tensor(x[:, g, cols], x[:, g, cols], pb(kb)[:], ALU.add).then_inc(s_xnew, 1)
                        else:
                            V.tensor_tensor(x[:, g, cols], x[:, g, cols], pb(kw)[:], ALU.mult).then_inc(*drain(kw))
                            dve.wait_ge(*saved(kw))
                            V.tensor_tensor(x[:, g, cols], x[:, g, cols], pb(kb)[:], ALU.add).then_inc(*drain(kb))
                dve.wait_ge(s_xnew, 2 * (2 * l + s) + 2)
                for hf in range(2):
                    dve.wait_ge(*saved(("ln", l, s, 1, hf)))

            def route(l):
                dve.wait_ge(*saved(("logits", l)))
                ch.then(V.tensor_scalar(aff[:], aff[:], 1.0, None, ALU.add))
                ch.then(V.reciprocal(aff[:], aff[:]))
                ch.then(V.tensor_tensor(sel[:].rearrange("p (g e) -> p g e", g=G), aff[:].rearrange(
                    "p (g e) -> p g e", g=G), rbias_b[:].unsqueeze(1).to_broadcast([P, G, N_EXP]), ALU.add))
                s4 = sel[:].rearrange("p (q j) -> p q j", j=PER_GRP)
                p6 = pairs[:].rearrange("p (q j) -> p q j", j=6)
                V.tensor_tensor(p6[:, :, 0:3], s4[:, :, 0:3], s4[:, :, 1:4], ALU.add)
                V.tensor_tensor(p6[:, :, 3:5], s4[:, :, 0:2], s4[:, :, 2:4], ALU.add)
                ch.then(V.tensor_tensor(p6[:, :, 5:6], s4[:, :, 0:1], s4[:, :, 3:4], ALU.add))
                ch.then(V.tensor_reduce(gsc[:], p6, AX.X, ALU.max))
                g4 = gsc[:].rearrange("p (g q) -> p g q", g=G)
                ch.then(V.tensor_reduce(gmx[:], g4, AX.X, ALU.max))
                gp = gpr[:].rearrange("p (g q) -> p g q", g=G)
                gs = gsel[:].rearrange("p (g q) -> p g q", g=G)
                ch.then(V.tensor_tensor(gp, g4, gmx[:].unsqueeze(2).to_broadcast([P, G, N_GRP]), ALU.is_equal))
                ch.then(V.tensor_tensor(gp, gp, cst(C_PRIO, N_GRP).unsqueeze(1).to_broadcast([P, G, N_GRP]), ALU.mult))
                ch.then(V.tensor_reduce(gmx[:], gp, AX.X, ALU.max))
                V.tensor_tensor(gs, gp, gmx[:].unsqueeze(2).to_broadcast([P, G, N_GRP]), ALU.is_equal)
                shape = [P, 8, PER_GRP, PER_GRP]
                sj, si = s4.unsqueeze(2).to_broadcast(shape), s4.unsqueeze(3).to_broadcast(shape)
                gt = rk_gt.rearrange("p (q i j) -> p q i j", q=8, i=PER_GRP)
                eq = rk_eq.rearrange("p (q i j) -> p q i j", q=8, i=PER_GRP)
                V.tensor_tensor(gt, sj, si, ALU.is_gt)
                ch.then(V.tensor_tensor(eq, sj, si, ALU.is_equal))
                low = cst(C_LOW, 16).unsqueeze(1).to_broadcast([P, 8, 16])
                e3, g3 = rk_eq.rearrange("p (q n) -> p q n", q=8), rk_gt.rearrange("p (q n) -> p q n", q=8)
                ch.then(V.tensor_tensor(e3, e3, low, ALU.mult))
                ch.then(V.tensor_tensor(g3, g3, e3, ALU.add))
                ch.then(V.tensor_reduce(chosen[:], rk_gt.rearrange("p (n j) -> p n j", j=PER_GRP), AX.X, ALU.add))
                c4 = chosen[:].rearrange("p (q j) -> p q j", j=PER_GRP)
                ch.then(V.tensor_scalar(chosen[:], chosen[:], 2.0, None, ALU.is_lt))
                V.tensor_tensor(c4, c4, gsel[:].unsqueeze(2).to_broadcast([P, 8, PER_GRP]),
                                ALU.mult).then_inc(s_ch, 1)
                dve.wait_ge(s_ch, l + 1)
                ch.then(V.tensor_tensor(wsel[:], aff[:], chosen[:], ALU.mult))
                w2 = wsel[:].rearrange("p (g e) -> p g e", g=G)
                ch.then(V.tensor_reduce(wden[:], w2, AX.X, ALU.add))
                ch.then(V.reciprocal(wden[:], wden[:]))
                ch.then(V.tensor_tensor(pg[:, 2:4, :], w2, wden[:].unsqueeze(2).to_broadcast([P, G, N_EXP]), ALU.mult))
                ch.then(V.tensor_scalar(wsel[:], chosen[:], -1000.0, 1000.0, ALU.mult, ALU.add))
                dve.wait_ge(*full(("pos", l)))
                out = pb(("pos", l))
                ch.then(V.tensor_tensor(pg[:, 0:2, :], w2, out[:, 0:32].rearrange("p (g e) -> p g e", g=G), ALU.add))
                V.tensor_reduce(cmax[:], out[:, 64:80], AX.X, ALU.max).then_inc(*drain(("pos", l)))
                dve.wait_ge(*saved(("pos", l)))
                V.tensor_copy(over[:], cmax[:]).then_inc(s_over, 1)

            def hidden(gu, order_sem, base, done):
                V.tensor_scalar(s_sb, e_sb, 1.0, None, ALU.add).then_inc(order_sem, 1)
                dve.wait_ge(order_sem, base + 1)
                V.reciprocal(s_sb, s_sb).then_inc(order_sem, 1)
                dve.wait_ge(order_sem, base + 2)
                V.tensor_tensor(t_sb, gu[:, 0:256], s_sb, ALU.mult).then_inc(order_sem, 1)
                dve.wait_ge(order_sem, base + 3)
                V.tensor_tensor(hid, t_sb, gu[:, 256:512], ALU.mult).then_inc(*done)

            def experts(l):
                with dve.Fori(0, N_EXP) as e:
                    dve.wait_ge(s_ge, e + (N_EXP * l + 1))
                    hidden(pb(("gu", l)), s_dve_e, e * 3 + 3 * N_EXP * l, drain(("gu", l)))
                    dve.wait_ge(*full(("ye", l), e))
                    V.tensor_copy(ye_sb, pb(("ye", l))[:]).then_inc(*drain(("ye", l)))

            def overflow(l):
                o = ov[l]
                dve.wait_ge(s_over, l + 1)
                most = dve.value_load(over[0:1, 0:1], min_val=0, max_val=G * P)
                with dve.If(most > SLOTS):
                    with dve.Fori(0, n_over) as s:
                        dve.wait_ge(o["e"], s + 1)
                        hidden(bank[4], o["dve"], s * 3, (o["hid"], 1))
                        dve.wait_ge(o["used"], s * 12 + 14)
                        V.tensor_copy(ye_sb, bank[7][:]).then_inc(o["ye"], 1)

            V.memset(rows[:], 0.0).then_inc(s_zero, 1)
            ch.then(V.memset(cwin.rearrange("p k w -> p (k w)"), 0.0))
            dve.wait_ge(s_cexp, 1)
            ch.then(V.tensor_scalar(cexp, cexp, 1.0, None, ALU.add))
            ch.then(V.reciprocal(cexp, cexp))
            ch.then(V.tensor_tensor(cwin[:, :, 24], cvec[:, 0, :], cexp[:, 0, :], ALU.mult))
            V.tensor_tensor(cwin[:, :, 25], cvec[:, 1, :], cexp[:, 1, :], ALU.mult).then_inc(s_cwin, 1)
            dve.wait_ge(s_load, SMALL_LOADS)
            dve.wait_ge(s_x, 32)
            for l in range(DEPTH):
                modulated(l, 0)
                if l == 0:
                    normalise_even()
                else:
                    normalise_odd()
                attention(l)
                layer_norm(l, 0)
                modulated(l, 1)
                route(l)
                experts(l)
                overflow(l)
                layer_norm(l, 1)

        @block.scalar
        def _(act):
            A = nc.scalar

            def copy_out(key, dst, src=None):
                act.wait_ge(*full(key))
                A.activation(dst, pb(key)[:] if src is None else src, ACT.Copy).then_inc(*drain(key))

            def modulated(l, s):
                for g in range(G):
                    for q in range(2):
                        copy_out(("hT", l, s, g, q), hT[:, g, 4 * q:4 * q + 4, :].rearrange("p k t -> p (k t)"))

            def projected(l):
                for b, (c0, c1) in enumerate(WIN[l]):
                    for g in range(G):
                        key = ("z", l, b, g)
                        dst, src = z[l][:, g, c0:c1], pb(key)[:, 0:c1 - c0]
                        if (l, b) in ((0, 1), (1, 0), (1, 1)):
                            dst = dst.rearrange("p (j v c) -> p j v c", j=4, v=2)
                            src = src.rearrange("p (v j c) -> p j v c", j=4, v=2)
                        copy_out(key, dst, src)

            def unit_exp(l, unit):
                u, kind, g, kv, heads = unit
                b, nh = u % 2, len(heads)
                nk = HALF // nh
                scale = (QK_A if kind == "mla" else HD) ** -0.5
                act.wait_ge(s_nm, 12 * l + u + 1)
                if u >= 2:
                    act.wait_ge(*full(("T", l, u - 2)))
                if l == 0 and kind == "gqa":
                    A.activation(sinke[b][:, 0:nh], sinke[b][:, 0:nh], ACT.Exp)
                for i in range(nh):
                    ins = A.activation(prob[b][:, i * nk:(i + 1) * nk], pb(("S", l, u))[:, i * nk:(i + 1) * nk],
                                       ACT.Exp, bias=negm[b][:, i:i + 1], scale=scale, accum_out=sume[b][:, i:i + 1])
                ins.then_inc(*drain(("S", l, u)))

            def attention(l):
                for group, seg in attention_units(l):
                    if group is not None:
                        g, quad = group
                        for b in range(1 + g):
                            copy_out(("kn", g, quad, b), kTa[0:NOPE_A, b * HALF:(b + 1) * HALF],
                                     pb(("kn", g, quad, b))[0:NOPE_A, :])
                        copy_out(("qaT", g, quad), qTa[0:QK_A].rearrange("p h t -> p (h t)"),
                                 pb(("qaT", g, quad))[0:QK_A, :])
                    unit_exp(l, seg[0])
                    for i, unit in enumerate(seg):
                        if i + 1 < len(seg):
                            unit_exp(l, seg[i + 1])
                        n = P * len(unit_chunks(l, unit))
                        copy_out(("O", l, unit[0]), out_T(l, unit[0])[:, 0:n], pb(("O", l, unit[0]))[:, 0:n])

            def layer_norm(l, s):
                for g in range(G):
                    for hf in range(2):
                        if g == 1:
                            act.wait_ge(*saved(("y", l, s, 0, hf)))
                        copy_out(("gate", l, s, g, hf), gcopy[hf])
                act.wait_ge(s_lnb, 2 * l + s + 1)
                for g in range(G):
                    A.activation(x[:, g, :], x[:, g, :], ACT.Identity, bias=lnnb[:, g:g + 1],
                                 scale=rstd[:, g:g + 1]).then_inc(s_norm, 1)

            def route(l):
                key = ("logits", l)
                act.wait_ge(*full(key))
                A.activation(aff[:], pb(key)[:, 0:32], ACT.Exp, scale=-1.0).then_inc(*drain(key))

            def gate_exp(l, e):
                act.wait_ge(*full(("gu", l), e))
                A.activation(e_sb, pb(("gu", l))[:, 0:256], ACT.Exp, scale=-1.0).then_inc(s_ge, 1)

            def save(key, e, dst):
                act.wait_ge(*full(key, e))
                A.activation(dst, pb(key)[:], ACT.Copy).then_inc(*drain(key))

            def experts(l):
                save(("xe", l), 0, xeT[0])
                with act.Fori(0, N_EXP // 3) as i:
                    for j in range(3):
                        e = i * 3 + j
                        gate_exp(l, e)
                        save(("xe", l), e + 1, xeT[(j + 1) % 3])
                        save(("tp", l), e, hp[j])
                gate_exp(l, N_EXP - 1)
                save(("tp", l), N_EXP - 1, hp[(N_EXP - 1) % 3])

            def overflow(l):
                o = ov[l]
                act.wait_ge(s_over, l + 1)
                most = act.value_load(over[0:1, 0:1], min_val=0, max_val=G * P)
                with act.If(most > SLOTS):
                    with act.Fori(0, n_over) as s:
                        act.wait_ge(o["xe"], s + 1)
                        A.activation(xeT[0], bank[5][:], ACT.Copy).then_inc(o["xeT"], 1)
                        act.wait_ge(o["used"], s * 12 + 10)
                        A.activation(e_sb, bank[4][:, 0:256], ACT.Exp, scale=-1.0).then_inc(o["e"], 1)
                        act.wait_ge(o["tp"], s + 1)
                        A.activation(hp[0], bank[6][:], ACT.Copy).then_inc(o["hp"], 1)

            act.dma_start(cvec[:, 0, :], i_["c_ctx"].rearrange("(p k) -> p k", k=KD)).then_inc(s_c, 16)
            act.dma_start(cvec[:, 1, :], i_["c"][0].rearrange("(p k) -> p k", k=KD)).then_inc(s_c, 16)
            act.wait_ge(s_zero, 1)
            act.dma_start(rows[0:DEPTH * N_MOD, :], i_["b_mod"].rearrange("l (c n) -> (l c) n", n=HALF)
                          ).then_inc(s_rows, 16)
            for j, name in enumerate(("ln_g", "ln_b")):
                act.dma_start(rows[LN_ROW + 8 * j:LN_ROW + 8 * j + 8, :],
                              i_[name].rearrange("l s (h n) -> (l s h) n", n=HALF)).then_inc(s_rows, 16)
            act.dma_start(const[:], i_["constants"]).then_inc(s_load, 16)
            for g, name in enumerate(("x_prompt", "x_sample")):
                act.dma_start(x[:, g, :], i_[name][0]).then_inc(s_x, 16)
            for dst, name in ((qn_b, "mla_q_norm"), (kvn_b, "mla_kv_norm"), (sink_b, "swa_sink"),
                              (cqn_b, "gqa_q_norm"), (ckn_b, "gqa_k_norm")):
                act.dma_start(dst[:], i_[name][0].partition_broadcast(P)).then_inc(s_load, 16)
            act.dma_start(rbias_b[:], i_["router_bias"].partition_broadcast(P)).then_inc(s_load, 16)
            act.dma_start(rw, i_["router_w"].rearrange("(k p) e -> p k e", p=P)).then_inc(s_load, 16)
            act.dma_start(cache_c[:, 0:KV_LORA], i_["cache_mla_ckv"][0, 0]).then_inc(s_cache, 16)
            act.dma_start(cache_c[:, KV_LORA:KV_LORA + ROPE_A], i_["cache_mla_kpe"][0, 0]).then_inc(s_cache, 16)
            act.dma_start(cache_kb, i_["cache_swa_k"][0, 0].rearrange("t h c -> t (h c)")).then_inc(s_cache, 16)
            act.dma_start(cache_vb, i_["cache_swa_v"][0, 0].rearrange("t h c -> t (h c)")).then_inc(s_cache, 16)
            act.wait_ge(s_c, 32)
            A.activation(cexp, cvec, ACT.Exp, scale=-1.0).then_inc(s_cexp, 1)

            for l in range(DEPTH):
                if l == 0:
                    copy_out(("modA", 0), modA[:])
                modulated(l, 0)
                projected(l)
                if l == 0:
                    zp = z[0][:, 0, :]
                    act.wait_ge(*saved(("z", 0, 1, 0)))
                    act.wait_ge(*saved(("z", 0, 2, 0)))
                    act.dma_start(o_["new_swa_k"][0, 0].rearrange("t h c -> t (h c)"),
                                  zp[:, Z_KB:Z_VB]).then_inc(s_out, 16)
                    act.dma_start(o_["new_swa_v"][0, 0].rearrange("t h c -> t (h c)"),
                                  zp[:, Z_VB:AB_IN]).then_inc(s_out, 16)
                    for g in range(G):
                        copy_out(("qT", 0, g, 0), qbT[:, g].rearrange("p j t -> p (j t)"))
                    act.wait_ge(s_zfin, 2)
                    act.dma_start(o_["new_mla_ckv"][0, 0], zp[:, Z_CKV:Z_KPE]).then_inc(s_out, 16)
                    act.dma_start(o_["new_mla_kpe"][0, 0], zp[:, Z_KPE:Z_QB]).then_inc(s_out, 16)
                    copy_out(("krT",), krT[NOPE_A:QK_A, :], pb(("krT",))[NOPE_A:QK_A, 0:384])
                else:
                    act.dma_start(cache_kc, i_["cache_gqa_k"][0, 0].rearrange("t h c -> t (h c)")
                                  ).then_inc(s_cache, 16)
                    act.dma_start(cache_vc, i_["cache_gqa_v"][0, 0].rearrange("t h c -> t (h c)")
                                  ).then_inc(s_cache, 16)
                    for g in range(G):
                        for b in range(len(WIN[1]) - 1):
                            act.wait_ge(*saved(("z", 1, b, g)))
                        A.activation(sq[:, g].rearrange("p h c -> p (h c)"), z[1][:, g, 0:Z_VC],
                                     ACT.Square).then_inc(s_sq, 1)
                    zp = z[1][:, 0, :]
                    act.wait_ge(*saved(("z", 1, 3, 0)))
                    act.dma_start(o_["new_gqa_v"][0, 0].rearrange("t h c -> t (h c)"),
                                  zp[:, Z_VC:C_IN]).then_inc(s_out, 16)
                    act.wait_ge(s_zfin, 3)
                    act.dma_start(o_["new_gqa_k"][0, 0].rearrange("t h c -> t (h c)"),
                                  zp[:, Z_KC:Z_VC]).then_inc(s_out, 16)
                    for g in range(G):
                        for a in range(2):
                            copy_out(("qT", 1, g, a), qTc[:, g, 4 * a:4 * a + 4].rearrange("p j t -> p (j t)"))
                attention(l)
                copy_out(("modB", l), modB[:])
                act.wait_ge(s_out, 64 if l == 0 else 96)
                layer_norm(l, 0)
                modulated(l, 1)
                route(l)
                if l == 0:
                    copy_out(("modA", 1), modA[:])
                experts(l)
                overflow(l)
                layer_norm(l, 1)

        @block.gpsimd
        def _(pool):
            Q = nc.gpsimd

            def inverse_root(n, cols):
                pool.wait_ge(s_stat, n)
                Q.tensor_tensor(rstd[:, 0:cols], ss[:, 0:cols], mhalf[:, 0:cols], ALU.pow).then_inc(s_rstd, 1)

            def rope_keys():
                pool.wait_ge(*saved(("krT",)))
                for g in range(G):
                    for quad in range(2):
                        nk = P * (1 + g)
                        pool.wait_ge(*full(("kn", g, quad, 0)))
                        Q.tensor_copy(kTa[NOPE_A:QK_A, 0:4 * nk].rearrange("p (h t) -> p h t", h=4),
                                      krT[NOPE_A:QK_A, P * g:P * g + nk].unsqueeze(1).to_broadcast([ROPE_A, 4, nk])
                                      ).then_inc(s_krb, 1)

            def onehots(dst):
                iota = cst(C_IOTA, SLOTS)
                for g in range(G):
                    Q.tensor_scalar(dst[:, g, 0:SLOTS], iota, cur[:, g:g + 1], None, ALU.is_equal)
                    for d in range(2):
                        last = Q.tensor_scalar(dst[:, g, SLOTS * (1 + d):SLOTS * (2 + d)], iota, cur[:, g:g + 1],
                                               cur[:, 2 + g:3 + g], ALU.is_equal, ALU.mult)
                return last

            def slots(l, e, j):
                Q.tensor_copy(cur[:], pg[:, :, e]).then_inc(s_pool, 1)
                pool.wait_ge(s_pool, e + (N_EXP * l + 1))
                b, t = turn[("tp", l)]
                pool.wait_ge(filled[b], e + (t - 2))
                pool.sem_inc(s_tick, 1)
                onehots(oh[j % 3]).then_inc(s_oh, 1)
                pool.wait_ge(s_oh, e + (N_EXP * l + 1))
                pool.sem_inc(s_tick, 1)

            def experts(l):
                pool.wait_ge(*saved(("pos", l)))
                with pool.Fori(0, N_EXP // 3) as i:
                    for j in range(3):
                        slots(l, i * 3 + j, j)
                slots(l, N_EXP - 1, N_EXP - 1)

            def overflow(l):
                o = ov[l]
                pool.wait_ge(s_over, l + 1)
                most = pool.value_load(over[0:1, 0:1], min_val=0, max_val=G * P)
                with pool.If(most > SLOTS):
                    pool.wait_ge(*full(("tp", l), N_EXP - 1))
                    with pool.Fori(0, N_EXP) as e:
                        for c in range(N_CHUNKS - 1):
                            s = e * (N_CHUNKS - 1) + c
                            Q.tensor_copy(cur[:], pg[:, :, e]).then_inc(o["pool"], 1)
                            pool.wait_ge(o["pool"], s * 2 + 1)
                            pool.sem_inc(s_tick, 1)
                            Q.tensor_scalar(cur[:, 0:2], cur[:, 0:2], -float(SLOTS * (c + 1)), None,
                                            ALU.add).then_inc(o["pool"], 1)
                            pool.wait_ge(o["pool"], s * 2 + 2)
                            pool.sem_inc(s_tick, 1)
                            onehots(oh[0]).then_inc(o["oh"], 1)
                            pool.wait_ge(o["oh"], s + 1)
                            pool.wait_ge(o["tp"], s + 1)
                            pool.sem_inc(s_tick, 1)

            Q.memset(mhalf[:], -0.5).then_inc(s_pool0, 1)
            pool.wait_ge(s_pool0, 1)
            pool.wait_ge(s_load, SMALL_LOADS)
            inverse_root(1, 4)
            rope_keys()
            for l in range(DEPTH):
                inverse_root(3 * l + 2, 2)
                experts(l)
                overflow(l)
                inverse_root(3 * l + 3, 2)
                if l == 0:
                    inverse_root(4, 2 * (H_C + KVH_C))


_INS = ["x_prompt", "x_sample", "c", "cache_mla_ckv", "cache_mla_kpe", "cache_swa_k", "cache_swa_v", "cache_gqa_k",
        "cache_gqa_v", "c_ctx", "w_mod", "b_mod", "ln_g", "ln_b", "w_in_ab", "mla_q_norm", "mla_w_uq", "mla_kv_norm",
        "mla_w_ukv", "swa_sink", "w_out_ab", "w_in_c", "gqa_q_norm", "gqa_k_norm", "w_out_c", "router_w",
        "router_bias", "exp_w_gate", "exp_w_up", "exp_w_down"]
_OUTS = [("y_prompt", (1, P, D)), ("y_sample", (1, P, D)), ("new_mla_ckv", (1, 1, P, KV_LORA)),
         ("new_mla_kpe", (1, 1, P, ROPE_A)), ("new_swa_k", (1, 1, P, KVH_B, HD)), ("new_swa_v", (1, 1, P, KVH_B, HD)),
         ("new_gqa_k", (1, 1, P, KVH_C, HD)), ("new_gqa_v", (1, 1, P, KVH_C, HD))]


def kernel(**inputs):
    import concourse.bacc as _bacc
    from concourse.bass_utils import run_bass_kernel_spmd as _run

    nc = _bacc.Bacc("TRN2", target_bir_lowering=False, num_devices=1)
    arrays, ins, outs = {}, {}, {}
    for name in _INS:
        a = np.ascontiguousarray(inputs[name])
        arrays[f"in_{name}"] = a
        ins[name] = nc.dram_tensor(f"in_{name}", a.shape, mybir.dt.from_np(a.dtype), kind="ExternalInput").ap()
    arrays["in_constants"] = shape_constants()
    ins["constants"] = nc.dram_tensor("in_constants", (P, C_COLS), F32, kind="ExternalInput").ap()
    for name, shape in _OUTS:
        outs[name] = nc.dram_tensor(f"out_{name}", shape, F32, kind="ExternalOutput").ap()
    hybrid_backbone(nc, ins, outs)
    r = _run(nc, [arrays], core_ids=[0])
    return tuple(r.results[0][f"out_{name}"] for name, _ in _OUTS)
```

```python
from contextlib import ExitStack

import numpy as np

import concourse.bass as bass
from concourse import mybir

F32 = mybir.dt.float32
I32 = mybir.dt.int32
ALU = mybir.AluOpType
ACT = mybir.ActivationFunctionType
AX = mybir.AxisListType

P = 128
G = 2
D = 1024
KD = D // P
DEPTH = 2
GRID_W = 64
ROPE_THETA = 10000.0
EPS = 1e-6
ALPHA = (2 * DEPTH) ** 0.25
HD = 64
Q_LORA, KV_LORA, ROPE_A, NOPE_A = 256, 128, 32, 64
QK_A = NOPE_A + ROPE_A
H_B, KVH_B = 8, 2
H_C, KVH_C = 16, 4
Z_CKV = Q_LORA
Z_KPE = Z_CKV + KV_LORA
Z_QB = Z_KPE + ROPE_A
Z_KB = Z_QB + H_B * HD
Z_VB = Z_KB + KVH_B * HD
AB_IN = Z_VB + KVH_B * HD
Z_KC = H_C * HD
Z_VC = Z_KC + KVH_C * HD
C_IN = Z_VC + KVH_C * HD
N_EXP, N_GRP, PER_GRP, F_EXP = 16, 4, 4, 512
SLOTS = 64
N_PAIR = N_EXP // 2
N_CHUNKS = G * P // SLOTS
HALF = 512
BLK = 4096
RING = 9

C_ID, C_TRI, C_ONE, C_SEL, C_BIAS, C_IOTA, C_PRIO, C_LOW, C_COSA, C_SINA, C_COSB, C_SINB = (
    0, 128, 256, 384, 416, 480, 544, 548, 564, 580, 596, 628)
C_COLS = 660
SMALL_LOADS = 7 * 16
N_MOD = 6 * D // HALF
MOD_PIECES = (range(0, 4), range(4, 8), range(8, 12))
LN_ROW = 32


def shape_constants():
    t = np.zeros((P, C_COLS), np.float32)
    i = np.arange(P)
    t[:, C_ID:C_ID + P] = np.eye(P)
    t[:, C_TRI:C_TRI + P] = i[:, None] < i[None, :]
    t[:, C_ONE:C_ONE + P] = 1.0
    t[:, C_SEL:C_SEL + 32] = (i[:, None] % 32) == np.arange(32)[None, :]
    for l in range(DEPTH):
        for c in range(N_MOD):
            t[l * N_MOD + c, C_BIAS + 32 * l + 2 * c:C_BIAS + 32 * l + 2 * c + 2] = 1.0
    t[:, C_IOTA:C_IOTA + SLOTS] = np.arange(SLOTS)
    t[:, C_PRIO:C_PRIO + N_GRP] = N_GRP - np.arange(N_GRP)
    low = (np.arange(PER_GRP)[None, :] < np.arange(PER_GRP)[:, None])
    t[:, C_LOW:C_LOW + PER_GRP * PER_GRP] = low.reshape(1, -1)
    for width, cc, cs in ((ROPE_A, C_COSA, C_SINA), (HD, C_COSB, C_SINB)):
        n_freq = width // 4
        inv = (1.0 / (ROPE_THETA ** (np.arange(n_freq, dtype=np.float32) / n_freq))).astype(np.float32)
        row, col = (i // GRID_W).astype(np.float32), (i % GRID_W).astype(np.float32)
        ang = np.concatenate([row[:, None] * inv, col[:, None] * inv], axis=-1)
        t[:, cc:cc + width // 2] = np.cos(ang)
        t[:, cs:cs + width // 2] = np.sin(ang)
    return t


def plan_blocks():
    order = [("mod", 0, c) for c in MOD_PIECES[0]] + [("win", 0, b) for b in range(3)]
    order += [("mod", 0, c) for c in MOD_PIECES[1]] + [("wout", 0, 1), ("lora", 0, 0), ("wout", 0, 0)]
    order += [("mod", 0, c) for c in MOD_PIECES[2]] + [("mod", 1, c) for c in MOD_PIECES[0]]
    order += [("exp", 0, b) for b in range(3 * N_EXP)]
    order += [("mod", 1, c) for c in MOD_PIECES[1]] + [("win", 1, b) for b in range(5)]
    order += [("mod", 1, c) for c in MOD_PIECES[2]] + [("wout", 1, b) for b in range(2)]
    order += [("exp", 1, b) for b in range(3 * N_EXP)]
    return order


WIN = {0: [(0, Z_QB), (Z_QB, Z_KB), (Z_KB, AB_IN)], 1: [(0, 512), (512, 1024), (1024, 1280), (1280, 1408), (1408, C_IN)]}


def attention_units(layer):
    units = []

    def add(kind, g, kv):
        for heads in ([(0, 1, 2, 3)] if g == 0 else [(0, 1), (2, 3)]):
            units.append((len(units), kind, g, kv, heads))

    for pair in range((KVH_B if layer == 0 else KVH_C) // 2):
        for g in range(G):
            for kv in (2 * pair, 2 * pair + 1):
                add("gqa", g, kv)
    if layer == 0:
        for g in range(G):
            for quad in range(2):
                add("mla", g, quad)
    return units


def attention_steps(layer):
    make = {0: [("kn", 0, 0), ("qa", 0)], 1: [("qaT", 0), ("va", 0)],
            2: [("kn", 1, 0), ("qa", 1)], 3: [("qaT", 1), ("va", 1)],
            4: [("kn", 2, 0), ("kn", 2, 1), ("qa", 2)], 5: [("qaT", 2)],
            6: [("va", 2), ("kn", 3, 0), ("kn", 3, 1), ("qa", 3)], 7: [("qaT", 3), ("va", 3)]}
    n = len(attention_units(layer))
    steps = [("S", 0), ("S", 1)]
    for u in range(n):
        steps.append(("T", u))
        if u > 0:
            steps.append(("Y", u - 1))
        steps.append(("V", u))
        if u + 2 < n:
            steps.append(("S", u + 2))
        if layer == 0:
            steps += make.get(u, [])
    return steps + [("Y", n - 1)]


def unit_chunks(layer, unit):
    _, kind, g, kv, heads = unit
    base = (4 if layer == 0 else 0) if kind == "gqa" else 0
    return [base + 2 * kv + heads[i] // 2 for i in range(0, len(heads), 2)]


class Turns:

    def __init__(self):
        self.count = [0] * 8
        self.at = {}

    def use(self, key, bank, n=1):
        assert key not in self.at
        self.at[key] = (bank, self.count[bank])
        self.count[bank] += n


def plan_turns():
    t = Turns()
    t.use(("mod", 0, 0), 7)
    for l in range(DEPTH):
        for s in range(2):
            for g in range(G):
                for hf in range(2):
                    t.use(("scale", l, s, g, hf), 2 * hf)
                    t.use(("shift", l, s, g, hf), 2 * hf + 1)
            for g in range(G):
                for q in range(2):
                    t.use(("hT", l, s, g, q), 4 + q)
            if s == 0:
                for b in range(len(WIN[l])):
                    for g in range(G):
                        t.use(("z", l, b, g), (2 * b + g) % 4)
                t.use(("mod", l, 1 + l), 3)
                if l == 0:
                    for g in range(G):
                        t.use(("qT", 0, g, 0), 4 + g)
                    t.use(("kT", 0, 0), 6)
                    t.use(("qlatT",), 7)
                    t.use(("ckvT",), 4)
                    t.use(("krT",), 5)
                else:
                    for g in range(G):
                        for j in range(2):
                            t.use(("qT", 1, g, j), 4 + j)
                    for j in range(2):
                        t.use(("kT", 1, j), 6 + j)
                for g in range(G):
                    for hf in range(2):
                        t.use(("y", l, 0, g, hf), 2 * g + hf)
                for step in attention_steps(l):
                    name, u = step[:2]
                    if name == "S":
                        t.use(("S", l, u), 4 + u % 2)
                    elif name == "T":
                        t.use(("T", l, u), 6)
                    elif name == "V":
                        t.use(("O", l, u), 7)
                    elif name == "kn":
                        t.use(step, 6 + step[2])
                    elif name in ("qa", "qaT"):
                        t.use(step, 6 if name == "qa" and u >= 2 else 7)
                    elif name == "va":
                        t.use(step, 6)
            else:
                t.use(("logits", l), 6)
                t.use(("pos", l), 7)
                if l == 0:
                    t.use(("mod", 1, 0), 4)
                for g in range(G):
                    for hf in range(2):
                        t.use(("y", l, 1, g, hf), 2 * g + hf)
                t.use(("gu", l), 4, N_EXP)
                for pair in range(N_PAIR):
                    for h in range(2):
                        t.use(("xe", l, pair, h), 5)
                    if pair > 0:
                        t.use(("ye1", l, pair - 1), 5)
                t.use(("ye1", l, N_PAIR - 1), 5)
                t.use(("tp", l), 6, N_EXP)
                t.use(("ye0", l), 7, N_PAIR)
            for g in range(G):
                for hf in range(2):
                    t.use(("gate", l, s, g, hf), 5 + hf)
            if l == 0:
                t.use(("mod", s, 2 - s), 4)
            for i, key in enumerate([(0, 0), (1, 0), (0, 1), (1, 1)]):
                t.use(("ln", l, s) + key, (7, 5, 6, 4)[i])
    return t.at


ROOTS = ["even"] + [("ln", 0, s, g) for s in range(2) for g in range(G)] + [("odd", g) for g in range(G)]
ROOTS += [("ln", 1, s, g) for s in range(2) for g in range(G)]


class Chain:

    def __init__(self, eng, sem):
        self.eng, self.sem, self.n, self.off = eng, sem, 0, 0

    def then(self, ins):
        self.n += 1
        ins.then_inc(self.sem, 1)
        self.eng.wait_ge(self.sem, self.off + self.n)


def hybrid_backbone(nc, i_, o_):
    turn = plan_turns()
    order = plan_blocks()
    index = {}
    for n, b in enumerate(order):
        index.setdefault(b, n)
    lora_n = index[("lora", 0, 0)]

    with ExitStack() as ctx:
        def sb(name, cols, dt=F32):
            return ctx.enter_context(nc.sbuf_tensor(name, [P, cols], dt))

        def sem(name):
            return ctx.enter_context(nc.semaphore(name))

        ring = sb("ring", RING * BLK)
        x = sb("x", G * D)[:].rearrange("p (g d) -> p g d", g=G)
        rows = sb("rows", HALF)
        mods = [sb(f"mod{l}", HALF) for l in range(DEPTH)]
        const = sb("const", C_COLS)
        cwin = sb("cwin", KD * 56)[:].rearrange("p (k w) -> p k w", w=56)
        qn_b = sb("qn_b", Q_LORA)
        kvn_b = sb("kvn_b", KV_LORA)
        sink_b = sb("sink_b", H_B)
        rbias_b = sb("rbias_b", N_EXP)
        cqn_b = sb("cqn_b", HD)
        ckn_b = sb("ckn_b", HD)
        rw = sb("rw", KD * N_EXP)[:].rearrange("p (k e) -> p k e", e=N_EXP)
        cvec = sb("cvec", 2 * KD)[:].rearrange("p (g k) -> p g k", g=G)
        cexp = sb("cexp", 2 * KD)[:].rearrange("p (g k) -> p g k", g=G)
        mhalf = sb("mhalf", 40)
        ss = sb("ss", 40)
        rstd = sb("rstd", 40)
        bnst = sb("bnst", G * 2 * 6)[:].rearrange("p (g h s) -> p g h s", g=G, h=2)
        bnmv = sb("bnmv", G * 2)[:].rearrange("p (g s) -> p g s", g=G)
        mx = [sb("mx%d" % b, 4) for b in range(2)]
        negm = [sb("negm%d" % b, 4) for b in range(2)]
        sume = [sb("sume%d" % b, 4) for b in range(2)]
        sinke = [sb("sinke%d" % b, 4) for b in range(2)]
        rsum = [sb("rsum%d" % b, 4) for b in range(2)]
        aff = sb("aff", 32)
        sel = sb("sel", 32)
        pairs = sb("pairs", 48)
        gsc = sb("gsc", 8)
        gmx = sb("gmx", 2)
        gpr = sb("gpr", 8)
        gsel = sb("gsel", 8)
        chosen = sb("chosen", 32)
        wsel = sb("wsel", 32)
        wden = sb("wden", 2)
        pg = sb("pg", 64)[:].rearrange("p (r e) -> p r e", e=N_EXP)
        cur = sb("cur", 8)[:].rearrange("p (r a) -> p r a", a=2)
        cmax = sb("cmax", 1)
        over = sb("over", 1, I32)
        arena = sb("arena", 10176)

        bank = [ctx.enter_context(nc.psum_tensor(f"bank{b}", [P, HALF], F32)) for b in range(8)]
        filled = [sem(f"filled{b}") for b in range(8)]
        drained = [sem(f"drained{b}") for b in range(8)]
        blk_ready = [sem(f"blk_ready{s}") for s in range(RING)]
        blk_free = sem("blk_free")
        s_load = sem("small_loads")
        s_cache = sem("cache_loads")
        s_zero = sem("rows_zeroed")
        s_rows = sem("rows_loaded")
        s_x = sem("x_loaded")
        s_const = sem("constants_loaded")
        s_c = sem("c_loaded")
        s_cexp = sem("cond_exp")
        s_cwin = sem("cond_windows")
        s_dve = sem("dve_order")
        s_pool = sem("pool_order")
        s_pool0 = sem("constants_set")
        s_tick = sem("pool_wait_met")
        s_dve_e = sem("dve_expert_order")
        s_stat = sem("stats_ready")
        s_rstd = sem("rstd_ready")
        s_zfin = sem("z_final")
        s_sq = sem("squares_ready")
        s_qa = sem("qa_ready")
        s_krb = sem("rope_keys_ready")
        s_nm = sem("negmax_ready")
        s_p = sem("probs_ready")
        s_xnew = sem("x_updated")
        s_affe = sem("affinity_exp")
        s_ch = sem("experts_chosen")
        s_over = sem("overflow_flag")
        s_oh = sem("onehot_ready")
        s_ge = sem("gate_exp_ready")
        s_out = sem("outputs_written")
        ov = [{n: sem(f"ov{l}_{n}") for n in (
            "piece0", "piece1", "used", "oh", "xe", "xeT", "e", "hid", "tp", "hp", "ye", "pool", "dve")}
            for l in range(DEPTH)]

        def cst(c, n, rows_=P):
            return const[0:rows_, c:c + n]

        ident = cst(C_ID, P)
        tri = cst(C_TRI, P)
        ones = cst(C_ONE, P)

        def ar(off, n):
            return arena[:, off:off + n]

        hr = ar(0, G * D).rearrange("p (g d) -> p g d", g=G)
        hT = ar(2048, G * D).rearrange("p (g k t) -> p g k t", g=G, k=KD)
        z = {0: ar(4096, G * AB_IN).rearrange("p (g c) -> p g c", g=G),
             1: ar(4096, G * C_IN).rearrange("p (g c) -> p g c", g=G)}
        rope_cos, rope_sin = ar(1024, 1280), ar(2304, 1280)
        qTc = ar(0, 2048).rearrange("p (g j t) -> p g j t", g=G, j=8)
        prob = [ar(2048 + HALF * b, HALF) for b in range(2)]
        probT = [ar(3072 + HALF * b, HALF) for b in range(2)]
        o0 = 4096 + G * AB_IN
        ckvT, krT = ar(o0, 384), ar(o0 + 384, 384)
        qlatT = ar(o0 + 768, 512).rearrange("p (g c t) -> p g c t", g=G, c=2)
        qbT = ar(o0 + 1280, 1024).rearrange("p (g j t) -> p g j t", g=G, j=4)
        kbT = ar(o0 + 2304, 384)
        cache_vb, cache_kb, cache_c = ar(o0 + 2688, 128), ar(o0 + 2816, 128), ar(o0 + 2944, 160)
        qa = ar(o0 + 2816, 384).rearrange("p (h c) -> p h c", h=4)
        oT_even = [ar(o0 + 3200 + 256 * b, 256) for b in range(2)]
        qa_cos, qa_sin = z[0][:, 0, 0:128], z[0][:, 0, 128:256]
        o1 = 4096 + G * C_IN
        kcT = ar(o1, 768).rearrange("p (j t) -> p j t", j=2)
        cache_kc, cache_vc = ar(o1 + 768, 256), ar(o1 + 1024, 256)
        oT_odd = [ar(o1 + 1280 + 256 * b, 256) for b in range(2)]
        sq = ar(0, 2560).rearrange("p (g h c) -> p g h c", g=G, c=HD)
        rk_gt, rk_eq = ar(2048, 128), ar(2176, 128)
        ov_w = [ar(2048 + 1024 * b, 1024) for b in range(2)]
        oh = [ar(2048 + HALF * b, HALF).rearrange("p (g c) -> p g c", g=G) for b in range(3)]
        xeT = [ar(4096 + D * b, D) for b in range(3)]
        ye_sb = ar(7168, D)
        e_sb, s_sb, hid, t_sb = (ar(8192 + 256 * i, 256) for i in range(4))
        hp = ar(9216, 768)
        oh_ov = xeT[1][:, 0:384].rearrange("p (g c) -> p g c", g=G)
        gcopy = [ar(5632 + HALF * b, HALF) for b in range(2)]
        upd = ar(6656, HALF)

        def block_ap(n):
            s = n % RING
            return ring[:, s * BLK:(s + 1) * BLK]

        def got(n, i=None):
            v = 16 * (n // RING + 1) + (16 if n % RING == lora_n % RING and n >= lora_n else 0)
            return blk_ready[n % RING], (v if i is None else i * 16 + v)

        def full(key, e=None):
            b, t = turn[key]
            return filled[b], (t + 1 if e is None else e + (t + 1))

        def saved(key, e=None):
            b, t = turn[key]
            return drained[b], (t + 1 if e is None else e + (t + 1))

        def room(eng, key, e=None):
            b, t = turn[key]
            if e is not None:
                eng.wait_ge(drained[b], e + t)
            elif t > 0:
                eng.wait_ge(drained[b], t)

        def root(key):
            return ROOTS.index(key) + 1

        def in_loop5(value, key, i):
            return value(key, None if i is None else i * 9)

        def room5(eng, key, i):
            room(eng, key, None if i is None else i * 9)

        def fill(key):
            return filled[turn[key][0]], 1

        def drain(key):
            return drained[turn[key][0]], 1

        def pb(key):
            return bank[turn[key][0]]

        def out_T(l, u):
            return (oT_even if l == 0 else oT_odd)[u % 2]

        w_mod = i_["w_mod"].rearrange("l (p k) c -> l p k c", k=KD)
        w_in = {0: i_["w_in_ab"][0].rearrange("(k p) c -> p k c", p=P),
                1: i_["w_in_c"][0].rearrange("(k p) c -> p k c", p=P)}
        w_out = {0: i_["w_out_ab"][0].rearrange("(k p) c -> p k c", p=P),
                 1: i_["w_out_c"][0].rearrange("(k p) c -> p k c", p=P)}
        w_gate = i_["exp_w_gate"].rearrange("l e (p k) f -> (l e) p (k f)", k=KD)
        w_up = i_["exp_w_up"].rearrange("l e (p k) f -> (l e) p (k f)", k=KD)
        w_down = i_["exp_w_down"].rearrange("l e (k p) c -> (l e) p k c", p=P)
        w_gate_k = i_["exp_w_gate"].rearrange("l e (p k) f -> (l e) k p f", k=KD)
        w_up_k = i_["exp_w_up"].rearrange("l e (p k) f -> (l e) k p f", k=KD)
        w_down_k = i_["exp_w_down"].rearrange("l e (k p) c -> (l e) k p c", p=P)

        uq = block_ap(lora_n)[:, 0:2 * 768].rearrange("p (c n) -> p c n", c=2)
        ukv = block_ap(lora_n)[:, 1536:2560].rearrange("p (h c) -> p h c", h=8)

        def kTa(group, b):
            return ar(HALF * b, HALF) if group % 2 == 0 else z[0][:, b, Z_QB:Z_KB]

        qTa = [v.rearrange("p (h t) -> p h t", h=4) for v in (ar(1024, HALF), block_ap(lora_n)[:, 2560:3072])]
        va = [ar(1536, HALF), block_ap(lora_n)[:, 3072:3584]]

        exp_n = [index[("exp", l, 0)] for l in range(DEPTH)]
        n_over = (N_CHUNKS - 1) * N_EXP

        block = ctx.enter_context(nc.Block())

        @block.sync
        def _(sp):
            def load_block(n):
                kind, l, b = order[n]
                dst = block_ap(n)
                if n >= RING:
                    sp.wait_ge(blk_free, n - RING + 1)
                if kind == "mod":
                    sp.dma_start(dst.rearrange("p (k c) -> p k c", k=KD),
                                 w_mod[l, :, :, b * HALF:(b + 1) * HALF]).then_inc(got(n)[0], 16)
                elif kind == "win":
                    c0, c1 = WIN[l][b]
                    sp.dma_start(dst[:, 0:KD * (c1 - c0)].rearrange("p (k c) -> p k c", k=KD),
                                 w_in[l][:, :, c0:c1]).then_inc(got(n)[0], 16)
                elif kind == "lora":
                    sp.dma_start(uq, i_["mla_w_uq"][0].rearrange("(c p) n -> p c n", p=P)).then_inc(got(n)[0], 16)
                    sp.dma_start(dst[:, 1536:2560], i_["mla_w_ukv"][0]).then_inc(got(n)[0], 16)
                else:
                    sp.dma_start(dst.rearrange("p (k c) -> p k c", k=4),
                                 w_out[l][:, 4 * b:4 * b + 4, :]).then_inc(got(n)[0], 16)

            def load_pair(l, j, i=None):
                n = exp_n[l] + 6 * j
                e = l * N_EXP + 2 * j if i is None else i * 6 + (l * N_EXP + 2 * j)
                for t, (src, a) in enumerate(((w_gate, 0), (w_up, 0), (w_gate, 1), (w_up, 1), (w_down, 0), (w_down, 1))):
                    m = n + t - RING + 1
                    sp.wait_ge(blk_free, m if i is None else i * 18 + m)
                    dst = block_ap(n + t)
                    if src is w_down:
                        dst = dst.rearrange("p (k c) -> p k c", k=4)
                    sp.dma_start(dst, src[e + a]).then_inc(got(n + t)[0], 16)

            def load_experts(l):
                with sp.Fori(0, 2) as i:
                    for j in range(3):
                        load_pair(l, j, i)
                for j in range(6, N_PAIR):
                    load_pair(l, j)

            def overflow(l):
                o = ov[l]
                sp.wait_ge(s_over, l + 1)
                most = sp.value_load(over[0:1, 0:1], min_val=0, max_val=G * P)
                with sp.If(most > SLOTS):
                    with sp.Fori(0, N_EXP) as e:
                        with sp.Fori(0, N_CHUNKS - 1) as c:
                            q = (e * (N_CHUNKS - 1) + c) * 12
                            for p in range(12):
                                sp.wait_ge(o["used"], q + (p + 1))
                                if p < 8:
                                    a, b = w_gate_k[e + l * N_EXP, p], w_up_k[e + l * N_EXP, p]
                                else:
                                    a = w_down_k[e + l * N_EXP, p - 8, :, 0:HALF]
                                    b = w_down_k[e + l * N_EXP, p - 8, :, HALF:D]
                                sp.dma_start(ov_w[p % 2][:, 0:HALF], a).then_inc(o[f"piece{p % 2}"], 16)
                                sp.dma_start(ov_w[p % 2][:, HALF:D], b).then_inc(o[f"piece{p % 2}"], 16)

            sp.dma_start(cvec[:, 0, :], i_["c_ctx"].rearrange("(p k) -> p k", k=KD)).then_inc(s_c, 16)
            sp.dma_start(cvec[:, 1, :], i_["c"][0].rearrange("(p k) -> p k", k=KD)).then_inc(s_c, 16)
            sp.dma_start(const[:], i_["constants"]).then_inc(s_const, 16)
            sp.wait_ge(s_zero, 1)
            sp.dma_start(rows[0:DEPTH * N_MOD, :], i_["b_mod"].rearrange("l (c n) -> (l c) n", n=HALF)
                         ).then_inc(s_rows, 16)
            for j, name in enumerate(("ln_g", "ln_b")):
                sp.dma_start(rows[LN_ROW + 8 * j:LN_ROW + 8 * j + 8, :],
                             i_[name].rearrange("l s (h n) -> (l s h) n", n=HALF)).then_inc(s_rows, 16)
            for n in range(exp_n[0]):
                load_block(n)
                if n == 3:
                    for g, name in enumerate(("x_prompt", "x_sample")):
                        sp.dma_start(x[:, g, :], i_[name][0]).then_inc(s_x, 16)
                if n == 6:
                    for dst, name in ((qn_b, "mla_q_norm"), (kvn_b, "mla_kv_norm"), (sink_b, "swa_sink"),
                                      (cqn_b, "gqa_q_norm"), (ckn_b, "gqa_k_norm")):
                        sp.dma_start(dst[:], i_[name][0].partition_broadcast(P)).then_inc(s_load, 16)
                    sp.dma_start(rbias_b[:], i_["router_bias"].partition_broadcast(P)).then_inc(s_load, 16)
                    sp.dma_start(rw, i_["router_w"].rearrange("(k p) e -> p k e", p=P)).then_inc(s_load, 16)
                    sp.dma_start(cache_c[:, 0:KV_LORA], i_["cache_mla_ckv"][0, 0]).then_inc(s_cache, 16)
                    sp.dma_start(cache_c[:, KV_LORA:KV_LORA + ROPE_A], i_["cache_mla_kpe"][0, 0]).then_inc(s_cache, 16)
                    sp.dma_start(cache_kb, i_["cache_swa_k"][0, 0].rearrange("t h c -> t (h c)")).then_inc(s_cache, 16)
                    sp.dma_start(cache_vb, i_["cache_swa_v"][0, 0].rearrange("t h c -> t (h c)")).then_inc(s_cache, 16)
            load_experts(0)
            overflow(0)
            for n in range(exp_n[0] + 3 * N_EXP, exp_n[1]):
                load_block(n)
            load_experts(1)
            overflow(1)
            for g, name in enumerate(("y_prompt", "y_sample")):
                for hf in range(2):
                    if g == 0:
                        sp.wait_ge(s_xnew, 4 * DEPTH - 1 + hf)
                    else:
                        sp.wait_ge(*saved(("ln", DEPTH - 1, 1, 1, hf)))
                    cols = slice(hf * HALF, (hf + 1) * HALF)
                    sp.dma_start(o_[name][0][:, cols], x[:, g, cols]).then_inc(s_out, 16)
            sp.wait_ge(s_out, 16 * 10)

        @block.tensor
        def _(pe):
            def bcast(key, lhs_col, rhs):
                room(pe, key)
                nc.tensor.matmul(pb(key)[:], lhs_col.to_broadcast([P, P]), rhs,
                                 start=True, stop=True).then_inc(*fill(key))

            def mod_row(key, l, part, g, hf):
                bcast(key, cst(C_SEL + 2 * (2 * part + hf) + g, 1), mods[l][:])

            def ln_row(key, l, s, which, hf):
                bcast(key, cst(C_ID + LN_ROW + 8 * which + 2 * (2 * l + s) + hf, 1), rows[:])

            def modulation(l, piece, free=0):
                key = ("mod", l, piece)
                room(pe, key)
                chunks = MOD_PIECES[piece]
                out = pb(key)
                for c in chunks:
                    n = index[("mod", l, c)]
                    pe.wait_ge(*got(n))
                    w = block_ap(n)
                    for k in range(KD):
                        j = k % 4
                        mm = nc.tensor.matmul(out[32 * j:32 * j + 32, :], cwin[:, k, 24 - 2 * c:56 - 2 * c],
                                              w[:, k * HALF:(k + 1) * HALF],
                                              start=(c == chunks[0] and k < 4), stop=False, skip_group_check=True)
                        if free and c == chunks[0] and k == 0:
                            mm.then_inc(blk_free, free)
                    mm.then_inc(blk_free, 1)
                bias = cst(C_BIAS + 32 * l, 32, DEPTH * N_MOD) if piece == 0 else \
                    tri[0:DEPTH * N_MOD, 0:1].to_broadcast([DEPTH * N_MOD, 32])
                nc.tensor.matmul(out[0:32, :], bias, rows[0:DEPTH * N_MOD, :],
                                 start=False, stop=True, skip_group_check=True).then_inc(*fill(key))

            def modulated(l, s):
                def pair(g, hf):
                    mod_row(("scale", l, s, g, hf), l, 3 * s + 1, g, hf)
                    mod_row(("shift", l, s, g, hf), l, 3 * s, g, hf)

                def turned(g, q):
                    key = ("hT", l, s, g, q)
                    room(pe, key)
                    pe.wait_ge(*saved(("shift", l, s, g, q)))
                    for k in range(4):
                        mm = nc.tensor.transpose(pb(key)[:, k * P:(k + 1) * P],
                                                 hr[:, g, (4 * q + k) * P:(4 * q + k + 1) * P], ident)
                        if (l, s, g, q, k) == (1, 1, 0, 0, 0):
                            mm.then_inc(blk_free, 1)
                    mm.then_inc(*fill(key))

                pair(0, 0)
                pair(0, 1)
                turned(0, 0)
                pair(1, 0)
                turned(0, 1)
                pair(1, 1)
                turned(1, 0)
                turned(1, 1)

            def project(l):
                for b, (c0, c1) in enumerate(WIN[l]):
                    n = index[("win", l, b)]
                    pe.wait_ge(*got(n))
                    w = block_ap(n)[:, 0:KD * (c1 - c0)].rearrange("p (k c) -> p k c", k=KD)
                    for g in range(G):
                        key = ("z", l, b, g)
                        room(pe, key)
                        if b == 0:
                            pe.wait_ge(*saved(("hT", l, 0, g, 1)))
                            pe.wait_ge(*saved(("hT", l, 0, g, 0)))
                        for k in range(KD):
                            mm = nc.tensor.matmul(pb(key)[:, 0:c1 - c0], hT[:, g, k, :], w[:, k, :],
                                                  start=(k == 0), stop=(k == KD - 1))
                        mm.then_inc(*fill(key))

            def transposes(key, ins, width=P):
                room(pe, key)
                for j, a in enumerate(ins):
                    mm = nc.tensor.transpose(pb(key)[0:width, j * P:(j + 1) * P], a, ident)
                mm.then_inc(*fill(key))

            def scores(l, unit):
                u, kind, g, kv, heads = unit
                key = ("S", l, u)
                room(pe, key)
                nk = P if g == 0 else 2 * P
                k0 = 0 if g == 0 else P
                group = 2 * g + kv
                if kind == "mla" and heads[0] == 0:
                    pe.wait_ge(s_krb, (1, 2, 4, 6)[group])
                    for b in range(1 + g):
                        pe.wait_ge(*saved(("kn", group, b)))
                    pe.wait_ge(*saved(("qaT", group)))
                for i, h in enumerate(heads):
                    if kind == "mla":
                        lhs = qTa[group % 2][0:QK_A, h, :]
                        c = h * nk
                        rhs = kTa(group, c // HALF)[0:QK_A, c % HALF:c % HALF + nk]
                    else:
                        r = HD * (kv % 2)
                        if l == 0:
                            lhs, rhs = qbT[r:r + HD, g, h, :], kbT[r:r + HD, k0:k0 + nk]
                        else:
                            lhs = qTc[r:r + HD, g, 4 * (kv // 2) + h, :]
                            rhs = kcT[r:r + HD, kv // 2, k0:k0 + nk]
                    mm = nc.tensor.matmul(pb(key)[:, i * nk:(i + 1) * nk], lhs, rhs, start=True, stop=True)
                mm.then_inc(*fill(key))

            def turn_probs(l, unit):
                u = unit[0]
                key = ("T", l, u)
                room(pe, key)
                pe.wait_ge(s_p, u + 1 + 12 * l)
                for j in range(4):
                    mm = nc.tensor.transpose(pb(key)[:, j * P:(j + 1) * P], prob[u % 2][:, j * P:(j + 1) * P], ident)
                mm.then_inc(*fill(key))

            def values(l, unit):
                u, kind, g, kv, heads = unit
                key = ("O", l, u)
                room(pe, key)
                pe.wait_ge(*saved(("T", l, u)))
                if kind == "mla":
                    pe.wait_ge(*saved(("va", 2 * g + kv)))
                nkt = 1 if g == 0 else 2
                for i, h in enumerate(heads):
                    half = HD * (h % 2)
                    for kt in range(nkt):
                        if kind == "mla":
                            v = va[kv % 2][:, kt * 256 + h * HD:kt * 256 + (h + 1) * HD]
                        elif l == 0:
                            v = z[0][:, g, Z_VB + kv * HD:Z_VB + (kv + 1) * HD] if kt == 0 else \
                                cache_vb[:, kv * HD:(kv + 1) * HD]
                        else:
                            v = z[1][:, g, Z_VC + kv * HD:Z_VC + (kv + 1) * HD] if kt == 0 else \
                                cache_vc[:, kv * HD:(kv + 1) * HD]
                        mm = nc.tensor.matmul(pb(key)[half:half + HD, (i // 2) * P:(i // 2 + 1) * P], v,
                                              probT[u % 2][:, (i * nkt + kt) * P:(i * nkt + kt + 1) * P],
                                              start=(kt == 0), stop=(kt == nkt - 1))
                mm.then_inc(*fill(key))

            begun = {}

            def out_project(l, unit):
                u, _, g, _, _ = unit
                pe.wait_ge(*saved(("O", l, u)))
                for ci, c in enumerate(unit_chunks(l, unit)):
                    n = index[("wout", l, c // 4)]
                    pe.wait_ge(*got(n))
                    w = block_ap(n)
                    first = (l, g) not in begun
                    begun[(l, g)] = begun.get((l, g), 0) + 1
                    for hf in range(2):
                        key = ("y", l, 0, g, hf)
                        if first:
                            room(pe, key)
                        mm = nc.tensor.matmul(pb(key)[:], out_T(l, u)[:, ci * P:(ci + 1) * P],
                                              w[:, (c % 4) * D + hf * HALF:(c % 4) * D + (hf + 1) * HALF],
                                              start=first, stop=(begun[(l, g)] == KD), skip_group_check=True)
                        if (u, ci, hf) == (6, 0, 0):
                            mm.then_inc(blk_free, 1)
                        if begun[(l, g)] == KD:
                            mm.then_inc(*fill(key))

            def mla_keys(key):
                _, group, b = key
                g, quad = group // 2, group % 2
                nk = P * (1 + g)
                per = HALF // nk
                room(pe, key)
                pe.wait_ge(*got(lora_n))
                for i in range(per):
                    mm = nc.tensor.matmul(pb(key)[0:NOPE_A, i * nk:(i + 1) * nk],
                                          ukv[:, 4 * quad + b * per + i, 0:NOPE_A], ckvT[:, P * g:P * g + nk],
                                          start=True, stop=True)
                mm.then_inc(*fill(key))

            def mla_queries(key):
                g, quad = key[1] // 2, key[1] % 2
                room(pe, key)
                for c in range(2):
                    mm = nc.tensor.matmul(pb(key)[:, 0:4 * QK_A], qlatT[:, g, c, :],
                                          uq[:, c, 4 * quad * QK_A:4 * (quad + 1) * QK_A],
                                          start=(c == 0), stop=(c == 1))
                mm.then_inc(*fill(key))

            def mla_values(key):
                g, quad = key[1] // 2, key[1] % 2
                room(pe, key)
                for kt in range(1 + g):
                    mm = nc.tensor.matmul(pb(key)[:, kt * 256:(kt + 1) * 256], ckvT[:, P * (g + kt):P * (g + kt + 1)],
                                          ukv[:, 4 * quad:4 * quad + 4, NOPE_A:NOPE_A + HD], start=True, stop=True)
                mm.then_inc(*fill(key))

            def mla_turn_queries(key):
                group = key[1]
                pe.wait_ge(*saved(("qa", group)))
                if group >= 2:
                    pe.wait_ge(s_qa, group - 1)
                transposes(key, [qa[:, h, :] for h in range(4)], width=QK_A)

            def attention(l):
                if l == 0:
                    pe.wait_ge(*saved(("z", 0, 2, 0)))
                    pe.wait_ge(*saved(("z", 0, 1, 0)))
                    for g in range(G):
                        if g == 1:
                            pe.wait_ge(s_zfin, 1)
                        transposes(("qT", 0, g, 0), [z[0][:, g, Z_QB + j * P:Z_QB + (j + 1) * P] for j in range(4)])
                    pe.wait_ge(s_cache, 64)
                    transposes(("kT", 0, 0), [z[0][:, 0, Z_KB:Z_VB], z[0][:, 1, Z_KB:Z_VB], cache_kb])
                    pe.wait_ge(s_zfin, 2)
                    transposes(("qlatT",), [z[0][:, g, c * P:(c + 1) * P] for g in range(G) for c in range(2)])
                    transposes(("ckvT",), [z[0][:, 0, Z_CKV:Z_KPE], z[0][:, 1, Z_CKV:Z_KPE], cache_c[:, 0:KV_LORA]])
                    transposes(("krT",), [z[0][:, 0, Z_KPE - NOPE_A:Z_QB], z[0][:, 1, Z_KPE - NOPE_A:Z_QB],
                                          cache_c[:, KV_LORA - NOPE_A:KV_LORA + ROPE_A]], width=QK_A)
                    pe.wait_ge(*saved(("qT", 0, 0, 0)))
                    pe.wait_ge(*saved(("qT", 0, 1, 0)))
                    pe.wait_ge(*saved(("kT", 0, 0)))
                else:
                    for g in range(G):
                        pe.wait_ge(s_zfin, 3 + g)
                        for a in range(2):
                            transposes(("qT", 1, g, a), [z[1][:, g, (4 * a + j) * P:(4 * a + j + 1) * P]
                                                          for j in range(4)])
                    pe.wait_ge(s_cache, 96)
                    for a in range(2):
                        c = slice(Z_KC + a * P, Z_KC + (a + 1) * P)
                        transposes(("kT", 1, a), [z[1][:, 0, c], z[1][:, 1, c], cache_kc[:, a * P:(a + 1) * P]])
                    for a in range(2):
                        pe.wait_ge(*saved(("qT", 1, 0, a)))
                        pe.wait_ge(*saved(("qT", 1, 1, a)))
                        pe.wait_ge(*saved(("kT", 1, a)))
                units = attention_units(l)
                do = {"S": lambda k: scores(l, units[k[1]]), "T": lambda k: turn_probs(l, units[k[1]]),
                      "V": lambda k: values(l, units[k[1]]), "Y": lambda k: out_project(l, units[k[1]]),
                      "kn": mla_keys, "qa": mla_queries, "va": mla_values, "qaT": mla_turn_queries}
                for step in attention_steps(l):
                    do[step[0]](step)

            def ln_rows(l, s, free=0):
                if s == 1:
                    pe.wait_ge(*saved(("mod", l, 2)))
                for g in range(G):
                    for hf in range(2):
                        mod_row(("gate", l, s, g, hf), l, 3 * s + 2, g, hf)
                if l == 0:
                    modulation(s, 2 - s, free)
                for hf in range(2):
                    ln_row(("ln", l, s, 0, hf), l, s, 0, hf)
                    ln_row(("ln", l, s, 1, hf), l, s, 1, hf)

            def route(l):
                key = ("logits", l)
                room(pe, key)
                for g in range(G):
                    pe.wait_ge(*saved(("hT", l, 1, g, 0)))
                    pe.wait_ge(*saved(("hT", l, 1, g, 1)))
                    for k in range(KD):
                        mm = nc.tensor.matmul(pb(key)[:, g * N_EXP:(g + 1) * N_EXP], hT[:, g, k, :], rw[:, k, :],
                                              start=(g == 0 and k == 0), stop=(k == KD - 1), skip_group_check=True)
                mm.then_inc(*fill(key))
                for g in range(G):
                    for hf in range(2):
                        room(pe, ("y", l, 1, g, hf))
                        nc.tensor.matmul(pb(("y", l, 1, g, hf))[:], tri[:, 0:1].to_broadcast([P, P]),
                                         const[:, 0:HALF], start=True, stop=False, skip_group_check=True)
                key = ("pos", l)
                room(pe, key)
                pe.wait_ge(s_ch, l + 1)
                out = pb(key)
                nc.tensor.matmul(out[:, 0:32], tri, chosen[:], start=True, stop=False, skip_group_check=True)
                nc.tensor.matmul(out[:, 16:32], ones, chosen[:, 0:16], start=False, stop=True, skip_group_check=True)
                nc.tensor.matmul(out[:, 64:80], ones, chosen[:, 0:16], start=False, stop=False, skip_group_check=True)
                nc.tensor.matmul(out[:, 64:80], ones, chosen[:, 16:32], start=False, stop=True,
                                 skip_group_check=True).then_inc(*fill(key))
                if l == 0:
                    modulation(1, 0)

            def gather(out, onehot, chunks, width):
                for i, k in enumerate(chunks):
                    for g in range(G):
                        h = hr[:, g, :].rearrange("p (m k) -> p k m", k=KD)[:, k, :]
                        mm = nc.tensor.matmul(out[:, i * width:(i + 1) * width], h, onehot[:, g, 0:width],
                                              start=(g == 0), stop=(g == 1))
                return mm

            def turn_hidden(out):
                for c in range(2):
                    mm = nc.tensor.transpose(out[:, c * P:(c + 1) * P], hid[:, c * P:(c + 1) * P], ident)
                    yield mm

            def turn_onehots(out, gated):
                for g in range(G):
                    mm = nc.tensor.transpose(out[:, 256 + g * P:256 + (g + 1) * P], gated[:, g, P:2 * P], ident)
                return mm

            def gate_up(l, a, n, i, e, b):
                room(pe, ("gu", l), e)
                pe.wait_ge(*got(n, i))
                pe.wait_ge(*got(n + 1, i))
                s0 = n % RING
                w = ring[:, s0 * BLK:(s0 + 2) * BLK].rearrange("p (w k f) -> p w k f", w=2, k=KD)
                for k in range(KD):
                    for hf in range(2):
                        mm = nc.tensor.matmul(pb(("gu", l))[SLOTS * hf:SLOTS * (hf + 1), :],
                                              xeT[b][:, k * P + SLOTS * a:k * P + SLOTS * (a + 1)],
                                              w[:, :, k, hf * 256:(hf + 1) * 256], start=(k == 0), stop=(k == KD - 1))
                mm.then_inc(*fill(("gu", l)))

            def spread_pair(l, hf, last=False):
                for g in range(G):
                    yield nc.tensor.matmul(pb(("y", l, 1, g, hf))[:], hp[:, HALF + g * P:HALF + (g + 1) * P],
                                           ye_sb[:, hf * HALF:(hf + 1) * HALF], start=False, stop=last,
                                           skip_group_check=True)

            def pair(l, j, i=None):
                last = i is None and j == N_PAIR - 1
                p = j if i is None else i * 3 + j
                n = exp_n[l] + 6 * j
                ri = None if i is None else i * 2
                first = i is None and j == 0
                b = j % 3
                pe.wait_ge(*in_loop5(saved, ("xe", l, j, 0), i))
                pe.wait_ge(*in_loop5(saved, ("xe", l, j, 1), i))
                for a in range(2):
                    e = p * 2 + a
                    gate_up(l, a, n + 2 * a, ri, e, b)
                    if not first:
                        if a == 0:
                            pe.wait_ge(*saved(("ye0", l), p - 1))
                        else:
                            pe.wait_ge(*in_loop5(saved, ("ye1", l, j - 1), i))
                        for q, mm in enumerate(spread_pair(l, a)):
                            if (a, q) == (0, 0):
                                mm.then_inc(blk_free, 2)
                    if not last:
                        if a == 0:
                            pe.wait_ge(s_oh, p + (N_PAIR * l + 2))
                        room5(pe, ("xe", l, j + 1, a), i)
                        gather(pb(("xe", l, 0, 0)), oh[(j + 1) % 3], range(4 * a, 4 * a + 4), P
                               ).then_inc(*fill(("xe", l, 0, 0)))
                    room(pe, ("tp", l), e)
                    pe.wait_ge(*saved(("gu", l), e))
                    for q, mm in enumerate(turn_hidden(pb(("tp", l)))):
                        if q == 0:
                            mm.then_inc(blk_free, 2)
                        if (a, q) == (0, 1):
                            mm.then_inc(*fill(("tp", l)))
                turn_onehots(pb(("tp", l)), oh[b]).then_inc(*fill(("tp", l)))
                pe.wait_ge(*saved(("tp", l), p * 2))
                pe.wait_ge(*saved(("tp", l), p * 2 + 1))
                pe.wait_ge(*got(n + 4, ri))
                pe.wait_ge(*got(n + 5, ri))
                for hf in range(2):
                    if hf == 0:
                        room(pe, ("ye0", l), p)
                        key = ("ye0", l)
                    else:
                        room5(pe, ("ye1", l, j), i)
                        key = ("ye1", l, 0)
                    for kf in range(4):
                        for a in range(2):
                            c = 256 * a + (kf % 2) * P + (kf // 2) * SLOTS
                            mm = nc.tensor.matmul(pb(key)[SLOTS * a:SLOTS * (a + 1), :], hp[:, c:c + SLOTS],
                                                  block_ap(n + 4 + a)[:, kf * D + hf * HALF:
                                                                          kf * D + (hf + 1) * HALF],
                                                  start=(kf == 0), stop=(kf == 3))
                    mm.then_inc(*fill(key))

            def experts(l):
                pe.wait_ge(s_oh, N_PAIR * l + 1)
                for h in range(2):
                    room(pe, ("xe", l, 0, h))
                    gather(pb(("xe", l, 0, h)), oh[0], range(4 * h, 4 * h + 4), P).then_inc(*fill(("xe", l, 0, h)))
                pair(l, 0)
                with pe.Fori(0, 2) as i:
                    for j in range(1, 4):
                        pair(l, j, i)
                pair(l, N_PAIR - 1)
                for hf in range(2):
                    pe.wait_ge(*(saved(("ye0", l), N_PAIR - 1) if hf == 0 else saved(("ye1", l, N_PAIR - 1))))
                    for g, mm in enumerate(spread_pair(l, hf, True)):
                        mm.then_inc(*fill(("y", l, 1, g, hf)))
                pe.sem_inc(blk_free, 2)

            def overflow(l):
                o = ov[l]
                pe.wait_ge(s_over, l + 1)
                most = pe.value_load(over[0:1, 0:1], min_val=0, max_val=G * P)
                with pe.If(most > SLOTS):
                    pe.sem_inc(o["used"], 2)
                    with pe.Fori(0, N_EXP) as e:
                        with pe.Fori(0, N_CHUNKS - 1) as c:
                            s = e * (N_CHUNKS - 1) + c
                            pe.wait_ge(o["oh"], s + 1)
                            gather(bank[5], oh_ov, range(KD), SLOTS).then_inc(o["xe"], 1)
                            pe.wait_ge(o["xeT"], s + 1)
                            for p in range(12):
                                if p == 8:
                                    pe.wait_ge(o["hid"], s + 1)
                                    for mm in turn_hidden(bank[6]):
                                        pass
                                    for g in range(G):
                                        mm = nc.tensor.transpose(bank[6][:, 256 + g * P:256 + (g + 1) * P],
                                                                 oh_ov[:, g, SLOTS:3 * SLOTS], ident)
                                    mm.then_inc(o["tp"], 1)
                                    pe.wait_ge(o["hp"], s + 1)
                                pe.wait_ge(o[f"piece{p % 2}"], s * 192 + (32 * (p // 2) + 32))
                                w = ov_w[p % 2]
                                for hf in range(2):
                                    if p < 8:
                                        mm = nc.tensor.matmul(
                                            bank[4][SLOTS * hf:SLOTS * (hf + 1), :],
                                            xeT[0][:, p * SLOTS:(p + 1) * SLOTS],
                                            w.rearrange("p (w f) -> p w f", w=2)[:, :, hf * 256:(hf + 1) * 256],
                                            start=(p == 0), stop=(p == 7))
                                    else:
                                        kf = p - 8
                                        lhs = hp[:, (kf % 2) * P + (kf // 2) * SLOTS:
                                                 (kf % 2) * P + (kf // 2 + 1) * SLOTS]
                                        mm = nc.tensor.matmul(bank[7][SLOTS * hf:SLOTS * (hf + 1), :], lhs,
                                                              w[:, hf * HALF:(hf + 1) * HALF],
                                                              start=(kf == 0), stop=(kf == 3))
                                mm.then_inc(o["used"], 1)
                            pe.wait_ge(o["ye"], s + 1)
                            for g in range(G):
                                for hf in range(2):
                                    r = SLOTS * hf
                                    nc.tensor.matmul(pb(("y", l, 1, g, hf))[:],
                                                     hp[r:r + SLOTS, 256 + g * P:256 + (g + 1) * P],
                                                     ye_sb[r:r + SLOTS, 0:HALF], start=False, stop=True,
                                                     skip_group_check=True)

            for l in range(DEPTH):
                if l == 0:
                    pe.wait_ge(s_cwin, 1)
                    pe.wait_ge(s_rows, 48)
                    pe.wait_ge(s_const, 16)
                    modulation(0, 0)
                pe.wait_ge(*saved(("mod", l, 0)))
                modulated(l, 0)
                project(l)
                modulation(l, 1 + l, free=len(WIN[l]))
                attention(l)
                pe.wait_ge(*saved(("mod", l, 1)))
                ln_rows(l, 0, free=2)
                pe.wait_ge(*saved(("mod", l, 2)))
                modulated(l, 1)
                if l == 0:
                    pe.wait_ge(s_load, SMALL_LOADS)
                route(l)
                experts(l)
                overflow(l)
                ln_rows(l, 1)

        @block.vector
        def _(dve):
            ch = Chain(dve, s_dve)
            V = nc.vector

            def modulate(l, s, g):
                for hf in range(2):
                    cols = slice(hf * HALF, (hf + 1) * HALF)
                    k_scale, k_shift = ("scale", l, s, g, hf), ("shift", l, s, g, hf)
                    dve.wait_ge(*full(k_scale))
                    V.scalar_tensor_tensor(out=hr[:, g, cols], in0=pb(k_scale)[:], scalar=1.0, in1=x[:, g, cols],
                                           op0=ALU.add, op1=ALU.mult).then_inc(*drain(k_scale))
                    dve.wait_ge(*saved(k_scale))
                    dve.wait_ge(*full(k_shift))
                    V.tensor_tensor(hr[:, g, cols], hr[:, g, cols], pb(k_shift)[:],
                                    ALU.add).then_inc(*drain(k_shift))

            def add_modulation(l, piece):
                key = ("mod", l, piece)
                dve.wait_ge(*full(key))
                V.tensor_tensor(mods[l][:], mods[l][:], pb(key)[:], ALU.add).then_inc(*drain(key))

            def rotate(v, cos, sin, tc, ts):
                n, half = v.shape[1], v.shape[3]
                tc = tc[:, 0:2 * n * half].rearrange("p (n a c) -> p n a c", n=n, a=2)
                ts = ts[:, 0:2 * n * half].rearrange("p (n a c) -> p n a c", n=n, a=2)
                for a in range(2):
                    V.tensor_tensor(tc[:, :, a], v[:, :, a], cos.unsqueeze(1).to_broadcast([P, n, half]), ALU.mult)
                    last = V.tensor_tensor(ts[:, :, a], v[:, :, a], sin.unsqueeze(1).to_broadcast([P, n, half]),
                                           ALU.mult)
                ch.then(last)
                ch.then(V.tensor_tensor(v[:, :, 0], tc[:, :, 0], ts[:, :, 1], ALU.subtract))
                return V.tensor_tensor(v[:, :, 1], tc[:, :, 1], ts[:, :, 0], ALU.add)

            def halves(v, n):
                return v.rearrange("p (n a c) -> p n a c", n=n, a=2)

            def normalise_even():
                for b in range(3):
                    for g in range(G):
                        dve.wait_ge(*saved(("z", 0, b, g)))
                zz = z[0]
                rotate(halves(zz[:, 1, Z_QB:Z_VB], H_B + KVH_B), cst(C_COSB, 32), cst(C_SINB, 32),
                       rope_cos, rope_sin).then_inc(s_zfin, 1)
                for g in range(G):
                    for i, (c0, c1) in enumerate(((0, Z_CKV), (Z_CKV, Z_KPE))):
                        ch.then(V.tensor_tensor_reduce(hr[:, 0, 0:c1 - c0], zz[:, g, c0:c1], zz[:, g, c0:c1], 1.0, 0.0,
                                                       ALU.mult, ALU.add, ss[:, 2 * g + i:2 * g + i + 1]))
                sv = ss[:, 0:4].rearrange("p (g i) -> p i g", i=2)
                ch.then(V.tensor_scalar(sv[:, 0], sv[:, 0], 1.0 / Q_LORA, EPS, ALU.mult, ALU.add))
                V.tensor_scalar(sv[:, 1], sv[:, 1], 1.0 / KV_LORA, EPS, ALU.mult, ALU.add).then_inc(s_stat, 1)
                add_modulation(0, 1)
                ch.then(rotate(halves(zz[:, 1, Z_KPE:Z_QB], 1), cst(C_COSA, 16), cst(C_SINA, 16),
                               rope_cos, rope_sin))
                dve.wait_ge(s_rstd, root("even"))
                for g in range(G):
                    for i, (c0, c1, w) in enumerate(((0, Z_CKV, qn_b), (Z_CKV, Z_KPE, kvn_b))):
                        ins = V.scalar_tensor_tensor(out=zz[:, g, c0:c1], in0=zz[:, g, c0:c1],
                                                     scalar=rstd[:, 2 * g + i:2 * g + i + 1], in1=w[:],
                                                     op0=ALU.mult, op1=ALU.mult)
                        if (g, i) == (1, 1):
                            ins.then_inc(s_zfin, 1)
                        else:
                            ch.then(ins)
                for key, dst in ((("kT", 0, 0), kbT), (("qlatT",), qlatT.rearrange("p g c t -> p (g c t)")),
                                 (("ckvT",), ckvT)):
                    dve.wait_ge(*full(key))
                    V.tensor_copy(dst, pb(key)[:, 0:dst.shape[1]]).then_inc(*drain(key))

            def normalise_odd():
                zz, n = z[1], H_C + KVH_C
                for g in range(G):
                    dve.wait_ge(s_sq, g + 1)
                    part = ss[:, n * g:n * (g + 1)]
                    ch.then(V.tensor_reduce(part, sq[:, g], AX.X, ALU.add))
                    V.tensor_scalar(part, part, 1.0 / HD, EPS, ALU.mult, ALU.add).then_inc(s_stat, 1)
                add_modulation(1, 2)
                for g in range(G):
                    dve.wait_ge(s_rstd, root(("odd", g)))
                    v = zz[:, g, 0:Z_VC].rearrange("p (h c) -> p h c", c=HD)
                    ch.then(V.tensor_tensor(v, v, rstd[:, n * g:n * (g + 1)].unsqueeze(2).to_broadcast([P, n, HD]),
                                            ALU.mult))
                    ch.then(V.tensor_tensor(v[:, 0:H_C], v[:, 0:H_C],
                                            cqn_b[:].unsqueeze(1).to_broadcast([P, H_C, HD]), ALU.mult))
                    ins = V.tensor_tensor(v[:, H_C:n], v[:, H_C:n],
                                          ckn_b[:].unsqueeze(1).to_broadcast([P, KVH_C, HD]), ALU.mult)
                    if g == 0:
                        ins.then_inc(s_zfin, 1)
                    else:
                        ch.then(ins)
                        rotate(halves(zz[:, 1, 0:Z_VC], n), cst(C_COSB, 32), cst(C_SINB, 32),
                               rope_cos, rope_sin).then_inc(s_zfin, 1)
                for a in range(2):
                    dve.wait_ge(*full(("kT", 1, a)))
                    V.tensor_copy(kcT[:, a, :], pb(("kT", 1, a))[:, 0:384]).then_inc(*drain(("kT", 1, a)))

            def unit_max(l, unit):
                u, kind, g, kv, heads = unit
                b, nh = u % 2, len(heads)
                scale = (QK_A if kind == "mla" else HD) ** -0.5
                dve.wait_ge(*full(("S", l, u)))
                ch.then(V.tensor_reduce(mx[b][:, 0:nh], pb(("S", l, u))[:].rearrange("p (h k) -> p h k", h=nh),
                                        AX.X, ALU.max))
                if l == 0 and kind == "gqa":
                    snk = sink_b[:, 4 * kv + heads[0]:4 * kv + heads[0] + nh]
                    ch.then(V.scalar_tensor_tensor(out=mx[b][:, 0:nh], in0=mx[b][:, 0:nh], scalar=scale, in1=snk,
                                                   op0=ALU.mult, op1=ALU.max))
                    ch.then(V.tensor_scalar(negm[b][:, 0:nh], mx[b][:, 0:nh], -1.0, None, ALU.mult))
                    V.tensor_tensor(sinke[b][:, 0:nh], snk, negm[b][:, 0:nh], ALU.add).then_inc(s_nm, 1)
                else:
                    V.tensor_scalar(negm[b][:, 0:nh], mx[b][:, 0:nh], -scale, None, ALU.mult).then_inc(s_nm, 1)

            def unit_normalise(l, unit):
                u, kind, g, kv, heads = unit
                b, nh = u % 2, len(heads)
                dve.wait_ge(*saved(("S", l, u)))
                if l == 0 and kind == "gqa":
                    ch.then(V.tensor_tensor(sume[b][:, 0:nh], sume[b][:, 0:nh], sinke[b][:, 0:nh], ALU.add))
                ch.then(V.reciprocal(rsum[b][:, 0:nh], sume[b][:, 0:nh]))
                pv = prob[b].rearrange("p (h k) -> p h k", h=nh)
                V.tensor_tensor(pv, pv, rsum[b][:, 0:nh].unsqueeze(2).to_broadcast([P, nh, HALF // nh]),
                                ALU.mult).then_inc(s_p, 1)

            def attention(l):
                units = attention_units(l)
                for step in attention_steps(l):
                    name, u = step[:2]
                    if name == "S":
                        unit_max(l, units[u])
                        if u == 0:
                            unit_normalise(l, units[0])
                    elif name == "T":
                        dve.wait_ge(*full(("T", l, u)))
                        V.tensor_copy(probT[u % 2], pb(("T", l, u))[:]).then_inc(*drain(("T", l, u)))
                        if u + 1 < len(units):
                            unit_normalise(l, units[u + 1])
                    elif name == "qa":
                        dve.wait_ge(*full(step))
                        V.tensor_copy(qa.rearrange("p h c -> p (h c)"), pb(step)[:, 0:4 * QK_A]).then_inc(*drain(step))
                        if u >= 2:
                            dve.wait_ge(*saved(step))
                            v = qa[:, :, NOPE_A:QK_A].rearrange("p h (a c) -> p h a c", a=2)
                            rotate(v, cst(C_COSA, 16), cst(C_SINA, 16), qa_cos, qa_sin).then_inc(s_qa, 1)
                    elif name == "va":
                        n = 256 * (1 + u // 2)
                        dve.wait_ge(*full(step))
                        V.tensor_copy(va[u % 2][:, 0:n], pb(step)[:, 0:n]).then_inc(*drain(step))

            def layer_norm(l, s, then=None):
                for g in range(G):
                    for hf in range(2):
                        cols = slice(hf * HALF, (hf + 1) * HALF)
                        key = ("y", l, s, g, hf)
                        dve.wait_ge(*full(key))
                        dve.wait_ge(*saved(("gate", l, s, g, hf)))
                        V.tensor_tensor(upd, pb(key)[:], gcopy[hf], ALU.mult).then_inc(*drain(key))
                        dve.wait_ge(*saved(key))
                        ch.then(V.scalar_tensor_tensor(out=x[:, g, cols], in0=x[:, g, cols], scalar=ALPHA, in1=upd,
                                                       op0=ALU.mult, op1=ALU.add))
                        last = V.bn_stats(bnst[:, g, hf, :], x[:, g, cols])
                    ch.then(last)
                    ch.then(V.bn_aggr(bnmv[:, g, :], bnst[:, g].rearrange("p h s -> p (h s)")))
                    V.tensor_scalar(ss[:, g:g + 1], bnmv[:, g, 1:2], EPS, None, ALU.add).then_inc(s_stat, 1)
                if l == 0:
                    add_modulation(s, 2 - s)
                for g in range(G):
                    for hf in range(2):
                        cols = slice(hf * HALF, (hf + 1) * HALF)
                        kw, kb = ("ln", l, s, 0, hf), ("ln", l, s, 1, hf)
                        dve.wait_ge(*full(kw))
                        ins = V.scalar_tensor_tensor(out=x[:, g, cols], in0=x[:, g, cols], scalar=bnmv[:, g, 0:1],
                                                     in1=pb(kw)[:], op0=ALU.subtract, op1=ALU.mult)
                        if g == 0:
                            ch.then(ins)
                        else:
                            ins.then_inc(*drain(kw))
                            dve.wait_ge(*saved(kw))
                        dve.wait_ge(s_rstd, root(("ln", l, s, g)))
                        dve.wait_ge(*full(kb))
                        ins = V.scalar_tensor_tensor(out=x[:, g, cols], in0=x[:, g, cols], scalar=rstd[:, g:g + 1],
                                                     in1=pb(kb)[:], op0=ALU.mult, op1=ALU.add)
                        if g == 0:
                            ins.then_inc(s_xnew, 1)
                        else:
                            ins.then_inc(*drain(kb))
                    for hf in range(2):
                        if g == 0:
                            dve.wait_ge(s_xnew, 2 * (2 * l + s) + hf + 1)
                        else:
                            dve.wait_ge(*saved(("ln", l, s, 1, hf)))
                    if then is not None:
                        then(g)

            def route(l):
                dve.wait_ge(*saved(("logits", l)))
                ch.then(V.tensor_scalar(aff[:], aff[:], 1.0, None, ALU.add))
                ch.then(V.reciprocal(aff[:], aff[:]))
                ch.then(V.tensor_tensor(sel[:].rearrange("p (g e) -> p g e", g=G), aff[:].rearrange(
                    "p (g e) -> p g e", g=G), rbias_b[:].unsqueeze(1).to_broadcast([P, G, N_EXP]), ALU.add))
                s4 = sel[:].rearrange("p (q j) -> p q j", j=PER_GRP)
                p6 = pairs[:].rearrange("p (q j) -> p q j", j=6)
                V.tensor_tensor(p6[:, :, 0:3], s4[:, :, 0:3], s4[:, :, 1:4], ALU.add)
                V.tensor_tensor(p6[:, :, 3:5], s4[:, :, 0:2], s4[:, :, 2:4], ALU.add)
                ch.then(V.tensor_tensor(p6[:, :, 5:6], s4[:, :, 0:1], s4[:, :, 3:4], ALU.add))
                ch.then(V.tensor_reduce(gsc[:], p6, AX.X, ALU.max))
                g4 = gsc[:].rearrange("p (g q) -> p g q", g=G)
                ch.then(V.tensor_reduce(gmx[:], g4, AX.X, ALU.max))
                gp = gpr[:].rearrange("p (g q) -> p g q", g=G)
                gs = gsel[:].rearrange("p (g q) -> p g q", g=G)
                ch.then(V.tensor_tensor(gp, g4, gmx[:].unsqueeze(2).to_broadcast([P, G, N_GRP]), ALU.is_equal))
                ch.then(V.tensor_tensor(gp, gp, cst(C_PRIO, N_GRP).unsqueeze(1).to_broadcast([P, G, N_GRP]), ALU.mult))
                ch.then(V.tensor_reduce(gmx[:], gp, AX.X, ALU.max))
                V.tensor_tensor(gs, gp, gmx[:].unsqueeze(2).to_broadcast([P, G, N_GRP]), ALU.is_equal)
                shape = [P, 8, PER_GRP, PER_GRP]
                sj, si = s4.unsqueeze(2).to_broadcast(shape), s4.unsqueeze(3).to_broadcast(shape)
                gt = rk_gt.rearrange("p (q i j) -> p q i j", q=8, i=PER_GRP)
                eq = rk_eq.rearrange("p (q i j) -> p q i j", q=8, i=PER_GRP)
                V.tensor_tensor(gt, sj, si, ALU.is_gt)
                ch.then(V.tensor_tensor(eq, sj, si, ALU.is_equal))
                low = cst(C_LOW, 16).unsqueeze(1).to_broadcast([P, 8, 16])
                e3, g3 = rk_eq.rearrange("p (q n) -> p q n", q=8), rk_gt.rearrange("p (q n) -> p q n", q=8)
                ch.then(V.tensor_tensor(e3, e3, low, ALU.mult))
                ch.then(V.tensor_tensor(g3, g3, e3, ALU.add))
                ch.then(V.tensor_reduce(chosen[:], rk_gt.rearrange("p (n j) -> p n j", j=PER_GRP), AX.X, ALU.add))
                c4 = chosen[:].rearrange("p (q j) -> p q j", j=PER_GRP)
                ch.then(V.tensor_scalar(chosen[:], chosen[:], 2.0, None, ALU.is_lt))
                V.tensor_tensor(c4, c4, gsel[:].unsqueeze(2).to_broadcast([P, 8, PER_GRP]),
                                ALU.mult).then_inc(s_ch, 1)
                dve.wait_ge(s_ch, l + 1)
                ch.then(V.tensor_tensor(wsel[:], aff[:], chosen[:], ALU.mult))
                w2 = wsel[:].rearrange("p (g e) -> p g e", g=G)
                ch.then(V.tensor_reduce(wden[:], w2, AX.X, ALU.add))
                ch.then(V.reciprocal(wden[:], wden[:]))
                ch.then(V.tensor_tensor(pg[:, 2:4, :], w2, wden[:].unsqueeze(2).to_broadcast([P, G, N_EXP]), ALU.mult))
                ch.then(V.tensor_scalar(wsel[:], chosen[:], -1000.0, 1000.0, ALU.mult, ALU.add))
                dve.wait_ge(*full(("pos", l)))
                out = pb(("pos", l))
                ch.then(V.tensor_tensor(pg[:, 0:2, :], w2, out[:, 0:32].rearrange("p (g e) -> p g e", g=G), ALU.add))
                V.tensor_reduce(cmax[:], out[:, 64:80], AX.X, ALU.max).then_inc(*drain(("pos", l)))
                dve.wait_ge(*saved(("pos", l)))
                V.tensor_copy(over[:], cmax[:]).then_inc(s_over, 1)

            def hidden(gu, order_sem, base, done):
                V.tensor_scalar(s_sb, e_sb, 1.0, None, ALU.add).then_inc(order_sem, 1)
                dve.wait_ge(order_sem, base + 1)
                V.reciprocal(s_sb, s_sb).then_inc(order_sem, 1)
                dve.wait_ge(order_sem, base + 2)
                V.tensor_tensor(t_sb, gu[:, 0:256], s_sb, ALU.mult).then_inc(order_sem, 1)
                dve.wait_ge(order_sem, base + 3)
                V.tensor_tensor(hid, t_sb, gu[:, 256:512], ALU.mult).then_inc(*done)

            def experts(l):
                with dve.Fori(0, N_PAIR) as p:
                    for a in range(2):
                        dve.wait_ge(s_ge, p * 2 + (N_EXP * l + a + 1))
                        hidden(pb(("gu", l)), s_dve_e, p * 6 + 3 * (N_EXP * l + a), drain(("gu", l)))
                    dve.wait_ge(*full(("ye0", l), p))
                    V.tensor_copy(ye_sb[:, 0:HALF], pb(("ye0", l))[:]).then_inc(*drain(("ye0", l)))

            def overflow(l):
                o = ov[l]
                dve.wait_ge(s_over, l + 1)
                most = dve.value_load(over[0:1, 0:1], min_val=0, max_val=G * P)
                with dve.If(most > SLOTS):
                    with dve.Fori(0, n_over) as s:
                        dve.wait_ge(o["e"], s + 1)
                        hidden(bank[4], o["dve"], s * 3, (o["hid"], 1))
                        dve.wait_ge(o["used"], s * 12 + 14)
                        V.tensor_copy(ye_sb[:, 0:HALF], bank[7][:]).then_inc(o["ye"], 1)

            V.memset(rows[:], 0.0).then_inc(s_zero, 1)
            ch.then(V.memset(cwin.rearrange("p k w -> p (k w)"), 0.0))
            dve.wait_ge(s_cexp, 1)
            ch.then(V.tensor_scalar(cexp, cexp, 1.0, None, ALU.add))
            ch.then(V.reciprocal(cexp, cexp))
            ch.then(V.tensor_tensor(cwin[:, :, 24], cvec[:, 0, :], cexp[:, 0, :], ALU.mult))
            V.tensor_tensor(cwin[:, :, 25], cvec[:, 1, :], cexp[:, 1, :], ALU.mult).then_inc(s_cwin, 1)
            dve.wait_ge(s_x, 32)
            dve.wait_ge(s_const, 16)
            for g in range(G):
                modulate(0, 0, g)
            dve.wait_ge(s_load, SMALL_LOADS)
            for l in range(DEPTH):
                if l == 0:
                    normalise_even()
                else:
                    normalise_odd()
                attention(l)
                layer_norm(l, 0, lambda g: modulate(l, 1, g))
                route(l)
                experts(l)
                overflow(l)
                layer_norm(l, 1, (lambda g: modulate(1, 0, g)) if l == 0 else None)

        @block.scalar
        def _(act):
            A = nc.scalar

            def copy_out(key, dst, src=None):
                act.wait_ge(*full(key))
                A.activation(dst, pb(key)[:] if src is None else src, ACT.Copy).then_inc(*drain(key))

            def modulated(l, s):
                for g in range(G):
                    for q in range(2):
                        copy_out(("hT", l, s, g, q), hT[:, g, 4 * q:4 * q + 4, :].rearrange("p k t -> p (k t)"))

            def projected(l):
                for b, (c0, c1) in enumerate(WIN[l]):
                    for g in range(G):
                        key = ("z", l, b, g)
                        dst, src = z[l][:, g, c0:c1], pb(key)[:, 0:c1 - c0]
                        if (l, b) in ((0, 1), (1, 0), (1, 1)):
                            dst = dst.rearrange("p (j v c) -> p j v c", j=4, v=2)
                            src = src.rearrange("p (v j c) -> p j v c", j=4, v=2)
                        copy_out(key, dst, src)

            def unit_exp(l, unit):
                u, kind, g, kv, heads = unit
                b, nh = u % 2, len(heads)
                nk = HALF // nh
                scale = (QK_A if kind == "mla" else HD) ** -0.5
                act.wait_ge(s_nm, 12 * l + u + 1)
                if u >= 2:
                    act.wait_ge(*full(("T", l, u - 2)))
                if l == 0 and kind == "gqa":
                    A.activation(sinke[b][:, 0:nh], sinke[b][:, 0:nh], ACT.Exp)
                for i in range(nh):
                    ins = A.activation(prob[b][:, i * nk:(i + 1) * nk], pb(("S", l, u))[:, i * nk:(i + 1) * nk],
                                       ACT.Exp, bias=negm[b][:, i:i + 1], scale=scale, accum_out=sume[b][:, i:i + 1])
                ins.then_inc(*drain(("S", l, u)))

            def attention(l):
                units = attention_units(l)
                for step in attention_steps(l):
                    name, u = step[:2]
                    if name == "S":
                        unit_exp(l, units[u])
                    elif name == "V":
                        n = P * len(unit_chunks(l, units[u]))
                        copy_out(("O", l, u), out_T(l, u)[:, 0:n], pb(("O", l, u))[:, 0:n])
                    elif name == "kn":
                        copy_out(step, kTa(u, step[2])[0:NOPE_A, :], pb(step)[0:NOPE_A, :])
                    elif name == "qaT":
                        copy_out(step, qTa[u % 2][0:QK_A].rearrange("p h t -> p (h t)"), pb(step)[0:QK_A, :])

            def gates(l, s):
                for g in range(G):
                    for hf in range(2):
                        if g == 1:
                            act.wait_ge(*saved(("y", l, s, 0, hf)))
                        copy_out(("gate", l, s, g, hf), gcopy[hf])

            def route(l):
                key = ("logits", l)
                act.wait_ge(*full(key))
                A.activation(aff[:], pb(key)[:, 0:32], ACT.Exp, scale=-1.0).then_inc(*drain(key))

            def gate_exp(l, e):
                act.wait_ge(*full(("gu", l), e))
                A.activation(e_sb, pb(("gu", l))[:, 0:256], ACT.Exp, scale=-1.0).then_inc(s_ge, 1)

            def pair(l, j, i=None):
                p = j if i is None else i * 3 + j
                for a in range(2):
                    gate_exp(l, p * 2 + a)
                    if not (i is None and j == N_PAIR - 1):
                        act.wait_ge(*in_loop5(full, ("xe", l, j + 1, a), i))
                        A.activation(xeT[(j + 1) % 3][:, a * HALF:(a + 1) * HALF], pb(("xe", l, 0, 0))[:],
                                     ACT.Copy).then_inc(*drain(("xe", l, 0, 0)))
                    act.wait_ge(*full(("tp", l), p * 2 + a))
                    n = 256 * (1 + a)
                    A.activation(hp[:, 256 * a:256 * a + n], pb(("tp", l))[:, 0:n], ACT.Copy).then_inc(*drain(("tp", l)))
                act.wait_ge(*in_loop5(full, ("ye1", l, j), i))
                A.activation(ye_sb[:, HALF:D], pb(("ye1", l, 0))[:], ACT.Copy).then_inc(*drain(("ye1", l, 0)))

            def experts(l):
                for h in range(2):
                    copy_out(("xe", l, 0, h), xeT[0][:, h * HALF:(h + 1) * HALF])
                pair(l, 0)
                with act.Fori(0, 2) as i:
                    for j in range(1, 4):
                        pair(l, j, i)
                pair(l, N_PAIR - 1)

            def overflow(l):
                o = ov[l]
                act.wait_ge(s_over, l + 1)
                most = act.value_load(over[0:1, 0:1], min_val=0, max_val=G * P)
                with act.If(most > SLOTS):
                    with act.Fori(0, n_over) as s:
                        act.wait_ge(o["xe"], s + 1)
                        A.activation(xeT[0][:, 0:HALF], bank[5][:], ACT.Copy).then_inc(o["xeT"], 1)
                        act.wait_ge(o["used"], s * 12 + 10)
                        A.activation(e_sb, bank[4][:, 0:256], ACT.Exp, scale=-1.0).then_inc(o["e"], 1)
                        act.wait_ge(o["tp"], s + 1)
                        A.activation(hp[:, 0:HALF], bank[6][:], ACT.Copy).then_inc(o["hp"], 1)

            act.wait_ge(s_c, 32)
            A.activation(cexp, cvec, ACT.Exp, scale=-1.0).then_inc(s_cexp, 1)

            for l in range(DEPTH):
                if l == 0:
                    copy_out(("mod", 0, 0), mods[0][:])
                modulated(l, 0)
                projected(l)
                if l == 0:
                    zp = z[0][:, 0, :]
                    act.wait_ge(*saved(("z", 0, 1, 0)))
                    act.wait_ge(*saved(("z", 0, 2, 0)))
                    act.dma_start(o_["new_swa_k"][0, 0].rearrange("t h c -> t (h c)"),
                                  zp[:, Z_KB:Z_VB]).then_inc(s_out, 16)
                    act.dma_start(o_["new_swa_v"][0, 0].rearrange("t h c -> t (h c)"),
                                  zp[:, Z_VB:AB_IN]).then_inc(s_out, 16)
                    for g in range(G):
                        copy_out(("qT", 0, g, 0), qbT[:, g].rearrange("p j t -> p (j t)"))
                    act.wait_ge(s_zfin, 2)
                    act.dma_start(o_["new_mla_ckv"][0, 0], zp[:, Z_CKV:Z_KPE]).then_inc(s_out, 16)
                    act.dma_start(o_["new_mla_kpe"][0, 0], zp[:, Z_KPE:Z_QB]).then_inc(s_out, 16)
                    copy_out(("krT",), krT[NOPE_A:QK_A, :], pb(("krT",))[NOPE_A:QK_A, 0:384])
                else:
                    act.dma_start(cache_kc, i_["cache_gqa_k"][0, 0].rearrange("t h c -> t (h c)")
                                  ).then_inc(s_cache, 16)
                    act.dma_start(cache_vc, i_["cache_gqa_v"][0, 0].rearrange("t h c -> t (h c)")
                                  ).then_inc(s_cache, 16)
                    for g in range(G):
                        for b in range(3):
                            act.wait_ge(*saved(("z", 1, b, g)))
                        A.activation(sq[:, g].rearrange("p h c -> p (h c)"), z[1][:, g, 0:Z_VC],
                                     ACT.Square).then_inc(s_sq, 1)
                    zp = z[1][:, 0, :]
                    for b in (3, 4):
                        act.wait_ge(*saved(("z", 1, b, 0)))
                    act.dma_start(o_["new_gqa_v"][0, 0].rearrange("t h c -> t (h c)"),
                                  zp[:, Z_VC:C_IN]).then_inc(s_out, 16)
                    act.wait_ge(s_zfin, 3)
                    act.dma_start(o_["new_gqa_k"][0, 0].rearrange("t h c -> t (h c)"),
                                  zp[:, Z_KC:Z_VC]).then_inc(s_out, 16)
                    for g in range(G):
                        for a in range(2):
                            copy_out(("qT", 1, g, a), qTc[:, g, 4 * a:4 * a + 4].rearrange("p j t -> p (j t)"))
                attention(l)
                act.wait_ge(s_out, 64 if l == 0 else 96)
                gates(l, 0)
                modulated(l, 1)
                route(l)
                if l == 0:
                    copy_out(("mod", 1, 0), mods[1][:])
                experts(l)
                overflow(l)
                gates(l, 1)

        @block.gpsimd
        def _(pool):
            Q = nc.gpsimd

            def inverse_root(key, c0, c1):
                n = root(key)
                pool.wait_ge(s_stat, n)
                Q.tensor_tensor(rstd[:, c0:c1], ss[:, c0:c1], mhalf[:, c0:c1], ALU.pow).then_inc(s_rstd, 1)

            def rope_keys():
                pool.wait_ge(*saved(("krT",)))
                for group in range(4):
                    g = group // 2
                    nk = P * (1 + g)
                    for b in range(1 + g):
                        pool.wait_ge(*full(("kn", group, b)))
                        Q.tensor_copy(kTa(group, b)[NOPE_A:QK_A, :].rearrange("p (h t) -> p h t", t=nk),
                                      krT[NOPE_A:QK_A, P * g:P * g + nk].unsqueeze(1).to_broadcast(
                                          [ROPE_A, HALF // nk, nk])).then_inc(s_krb, 1)

            def onehots(dst, a, copies, step):
                iota = cst(C_IOTA, SLOTS)
                c0 = SLOTS * a
                for g in range(G):
                    Q.tensor_scalar(dst[:, g, c0:c0 + SLOTS], iota, cur[:, g, a:a + 1], None, ALU.is_equal)
                    for d in range(copies):
                        c = c0 + step + SLOTS * d
                        last = Q.tensor_scalar(dst[:, g, c:c + SLOTS], iota, cur[:, g, a:a + 1],
                                               cur[:, 2 + g, a:a + 1], ALU.is_equal, ALU.mult)
                return last

            def slots(l, p, j):
                Q.tensor_copy(cur, pg[:, :, bass.ds(p * 2, 2)] if not isinstance(p, int) else
                              pg[:, :, 2 * p:2 * p + 2]).then_inc(s_pool, 1)
                pool.wait_ge(s_pool, p + (N_PAIR * l + 1))
                b, t = turn[("tp", l)]
                pool.wait_ge(filled[b], p * 2 + (t - 4))
                pool.sem_inc(s_tick, 1)
                onehots(oh[j % 3], 0, 1, P)
                onehots(oh[j % 3], 1, 1, P).then_inc(s_oh, 1)
                pool.wait_ge(s_oh, p + (N_PAIR * l + 1))
                pool.sem_inc(s_tick, 1)

            def experts(l):
                pool.wait_ge(*saved(("pos", l)))
                with pool.Fori(0, 2) as i:
                    for j in range(3):
                        slots(l, i * 3 + j, j)
                for p in (6, 7):
                    slots(l, p, p)

            def overflow(l):
                o = ov[l]
                pool.wait_ge(s_over, l + 1)
                most = pool.value_load(over[0:1, 0:1], min_val=0, max_val=G * P)
                with pool.If(most > SLOTS):
                    pool.wait_ge(*full(("tp", l), N_EXP - 1))
                    with pool.Fori(0, N_EXP) as e:
                        for c in range(N_CHUNKS - 1):
                            s = e * (N_CHUNKS - 1) + c
                            Q.tensor_copy(cur[:, :, 0], pg[:, :, e]).then_inc(o["pool"], 1)
                            pool.wait_ge(o["pool"], s * 2 + 1)
                            pool.sem_inc(s_tick, 1)
                            Q.tensor_scalar(cur[:, 0:2, 0], cur[:, 0:2, 0], -float(SLOTS * (c + 1)), None,
                                            ALU.add).then_inc(o["pool"], 1)
                            pool.wait_ge(o["pool"], s * 2 + 2)
                            pool.sem_inc(s_tick, 1)
                            onehots(oh_ov, 0, 2, SLOTS).then_inc(o["oh"], 1)
                            pool.wait_ge(o["oh"], s + 1)
                            pool.wait_ge(o["tp"], s + 1)
                            pool.sem_inc(s_tick, 1)

            Q.memset(mhalf[:], -0.5).then_inc(s_pool0, 1)
            pool.wait_ge(s_pool0, 1)
            inverse_root("even", 0, 4)
            rope_keys()
            pool.wait_ge(s_const, 16)
            for l in range(DEPTH):
                for g in range(G):
                    inverse_root(("ln", l, 0, g), g, g + 1)
                experts(l)
                overflow(l)
                for g in range(G):
                    inverse_root(("ln", l, 1, g), g, g + 1)
                if l == 0:
                    n = H_C + KVH_C
                    for g in range(G):
                        inverse_root(("odd", g), n * g, n * (g + 1))


_INS = ["x_prompt", "x_sample", "c", "cache_mla_ckv", "cache_mla_kpe", "cache_swa_k", "cache_swa_v", "cache_gqa_k",
        "cache_gqa_v", "c_ctx", "w_mod", "b_mod", "ln_g", "ln_b", "w_in_ab", "mla_q_norm", "mla_w_uq", "mla_kv_norm",
        "mla_w_ukv", "swa_sink", "w_out_ab", "w_in_c", "gqa_q_norm", "gqa_k_norm", "w_out_c", "router_w",
        "router_bias", "exp_w_gate", "exp_w_up", "exp_w_down"]
_OUTS = [("y_prompt", (1, P, D)), ("y_sample", (1, P, D)), ("new_mla_ckv", (1, 1, P, KV_LORA)),
         ("new_mla_kpe", (1, 1, P, ROPE_A)), ("new_swa_k", (1, 1, P, KVH_B, HD)), ("new_swa_v", (1, 1, P, KVH_B, HD)),
         ("new_gqa_k", (1, 1, P, KVH_C, HD)), ("new_gqa_v", (1, 1, P, KVH_C, HD))]


def kernel(**inputs):
    import concourse.bacc as _bacc
    from concourse.bass_utils import run_bass_kernel_spmd as _run

    nc = _bacc.Bacc("TRN2", target_bir_lowering=False, num_devices=1)
    arrays, ins, outs = {}, {}, {}
    for name in _INS:
        a = np.ascontiguousarray(inputs[name])
        arrays[f"in_{name}"] = a
        ins[name] = nc.dram_tensor(f"in_{name}", a.shape, mybir.dt.from_np(a.dtype), kind="ExternalInput").ap()
    arrays["in_constants"] = shape_constants()
    ins["constants"] = nc.dram_tensor("in_constants", (P, C_COLS), F32, kind="ExternalInput").ap()
    for name, shape in _OUTS:
        outs[name] = nc.dram_tensor(f"out_{name}", shape, F32, kind="ExternalOutput").ap()
    hybrid_backbone(nc, ins, outs)
    r = _run(nc, [arrays], core_ids=[0])
    return tuple(r.results[0][f"out_{name}"] for name, _ in _OUTS)
```
